# Optimizing a Trainium2 kernel written in Bass

```python
import math
import jax, jax.numpy as jnp
from jax import lax
import numpy as np
import jax
import jax.numpy as jnp

D_MODEL = 1024
BATCH = 1
SEQ = 256
DEPTH = 2

GRID_W = 64
HEAD_DIM = 128
ATTN_WIDTH = D_MODEL
N_HEADS = ATTN_WIDTH // HEAD_DIM
N_KV_HEADS = 2
GROUP = N_HEADS // N_KV_HEADS
KV_WIDTH = N_KV_HEADS * HEAD_DIM
Q_BLOCK = 128
ROPE_THETA = 10000.0
ROPE_HALF = HEAD_DIM // 2
POOL_WINDOWS = (2, 4, 8, 16)
N_POOL_GROUPS = 4
POOL_WIDTH = D_MODEL // 2
POOL_GROUP_DIM = POOL_WIDTH // N_POOL_GROUPS
IN_COLS = ATTN_WIDTH + 2 * KV_WIDTH + POOL_WIDTH + 2 * D_MODEL
N_PEER_HEADS = 8
PEER_QUERY_DIM = 512
SUBKEY_DIM = PEER_QUERY_DIM // 2
N_KEYS = 128
N_EXPERTS = N_KEYS * N_KEYS
PEER_TOPK = 16
TOKEN_BLOCK = 128
N_ADA = 6
EPS = 1e-6


def rms_norm(x, w):
    xf = x.astype(jnp.float32)
    y = xf * lax.rsqrt(jnp.mean(xf * xf, axis=-1, keepdims=True) + EPS)
    return (y * w.astype(jnp.float32)).astype(x.dtype)

def modulate(xn, shift, scale):
    return xn * (1.0 + scale[:, None, :]) + shift[:, None, :]

def axial_rope_angles(seq_len):
    rows = seq_len // GRID_W
    t = jnp.arange(rows * GRID_W)
    row = (t // GRID_W).astype(jnp.float32)
    col = (t % GRID_W).astype(jnp.float32)
    inv = 1.0 / (ROPE_THETA ** (jnp.arange(0, ROPE_HALF, 2, dtype=jnp.float32) / ROPE_HALF))
    return row[:, None] * inv, col[:, None] * inv

def rotate_half_dims(xh, ang):
    half = ROPE_HALF // 2
    cos = jnp.cos(ang)[None, :, None, :]
    sin = jnp.sin(ang)[None, :, None, :]
    xf = xh.astype(jnp.float32)
    x1, x2 = xf[..., :half], xf[..., half:]
    return jnp.concatenate([x1 * cos - x2 * sin, x2 * cos + x1 * sin], axis=-1).astype(xh.dtype)

def apply_axial_rope(x, ang_r, ang_c):
    return jnp.concatenate([rotate_half_dims(x[..., :ROPE_HALF], ang_r),
                            rotate_half_dims(x[..., ROPE_HALF:], ang_c)], axis=-1)

def blocked_bidirectional_gqa(q, k, v):
    B, S = q.shape[0], q.shape[1]
    nb = S // Q_BLOCK
    scale = 1.0 / math.sqrt(HEAD_DIM)
    qb = q.reshape(B, nb, Q_BLOCK, N_KV_HEADS, GROUP, HEAD_DIM).swapaxes(0, 1)

    def one_block(qblk):
        s = jnp.einsum('bqkgd,bskd->bkgqs', qblk, k).astype(jnp.float32) * scale
        p = jax.nn.softmax(s, axis=-1).astype(v.dtype)
        return jnp.einsum('bkgqs,bskd->bqkgd', p, v)

    ob = lax.map(one_block, qb)
    return ob.swapaxes(0, 1).reshape(B, S, N_HEADS * HEAD_DIM)

def multiscale_pool(u, pool_mix_w, pool_scale):
    B, S, _ = u.shape
    ug = u.reshape(B, S, N_POOL_GROUPS, POOL_GROUP_DIM).astype(jnp.float32)
    t = jnp.arange(S)
    outs = []
    for gi, w in enumerate(POOL_WINDOWS):
        xg = ug[:, :, gi, :]
        csum = jnp.concatenate([jnp.zeros((B, 1, POOL_GROUP_DIM), jnp.float32),
                                jnp.cumsum(xg, axis=1)], axis=1)
        lo = jnp.clip(t - w // 2, 0, S)
        hi = jnp.clip(t + w // 2, 0, S)
        cnt = (hi - lo).astype(jnp.float32)[None, :, None]
        outs.append((csum[:, hi] - csum[:, lo]) / cnt - xg)
    m = jnp.stack(outs, axis=2).astype(u.dtype)
    mixed = jnp.einsum('bsgc,gcd->bsgd', m, pool_mix_w).reshape(B, S, POOL_WIDTH)
    return mixed * pool_scale

def peer_ffn(xm, w_query, sub_keys, expert_u, expert_v):
    B, S, D = xm.shape
    nb = S // TOKEN_BLOCK
    xb = xm.reshape(B, nb, TOKEN_BLOCK, D).swapaxes(0, 1)

    def one_block(xblk):
        q = (xblk @ w_query).reshape(B, TOKEN_BLOCK, N_PEER_HEADS, 2, SUBKEY_DIM)
        s = jnp.einsum('bthpd,hpnd->bthpn', q, sub_keys).astype(jnp.float32)
        vals, idx = lax.top_k(s, PEER_TOPK)
        cand = (vals[..., 0, :, None] + vals[..., 1, None, :]).reshape(B, TOKEN_BLOCK, N_PEER_HEADS, PEER_TOPK * PEER_TOPK)
        cand_idx = (idx[..., 0, :, None] * N_KEYS + idx[..., 1, None, :]).reshape(B, TOKEN_BLOCK, N_PEER_HEADS, PEER_TOPK * PEER_TOPK)
        top_s, pos = lax.top_k(cand, PEER_TOPK)
        eidx = jnp.take_along_axis(cand_idx, pos, axis=-1)
        g = jax.nn.softmax(top_s, axis=-1).astype(xblk.dtype)
        u = expert_u[eidx]
        h = jnp.einsum('btd,bthkd->bthk', xblk, u)
        act = jax.nn.gelu(h, approximate=False) * g
        return jnp.einsum('bthk,bthkd->btd', act, expert_v[eidx])

    yb = lax.map(one_block, xb)
    return yb.swapaxes(0, 1).reshape(B, S, D)

def first_inputs(seed: int = 0) -> dict:
    key = jax.random.key(seed)
    ks = jax.random.split(key, 20)
    f32 = jnp.float32
    nrm = lambda k, shape, s: (jax.random.normal(k, shape, f32) * s)
    return {
        "x": nrm(ks[0], (BATCH, SEQ, D_MODEL), 1.0),
        "c": nrm(ks[1], (BATCH, D_MODEL), 1.0),
        "ada_w": nrm(ks[2], (DEPTH, D_MODEL, N_ADA * D_MODEL), 0.5 * D_MODEL ** -0.5),
        "ada_b": nrm(ks[3], (DEPTH, N_ADA * D_MODEL), 0.01),
        "norm_mix_w": 1.0 + nrm(ks[4], (DEPTH, D_MODEL), 0.05),
        "w_in": nrm(ks[5], (DEPTH, D_MODEL, IN_COLS), D_MODEL ** -0.5),
        "q_norm_w": 1.0 + nrm(ks[6], (DEPTH, HEAD_DIM), 0.05),
        "k_norm_w": 1.0 + nrm(ks[7], (DEPTH, HEAD_DIM), 0.05),
        "w_attn_o": nrm(ks[8], (DEPTH, ATTN_WIDTH, D_MODEL), ATTN_WIDTH ** -0.5),
        "pool_mix_w": nrm(ks[9], (DEPTH, N_POOL_GROUPS, POOL_GROUP_DIM, POOL_GROUP_DIM), POOL_GROUP_DIM ** -0.5),
        "pool_scale": 1.0 + nrm(ks[10], (DEPTH, POOL_WIDTH), 0.05),
        "w_pool_o": nrm(ks[11], (DEPTH, POOL_WIDTH, D_MODEL), POOL_WIDTH ** -0.5),
        "w_out": nrm(ks[12], (DEPTH, D_MODEL, D_MODEL), D_MODEL ** -0.5),
        "norm_ffn_w": 1.0 + nrm(ks[13], (DEPTH, D_MODEL), 0.05),
        "w_query": nrm(ks[14], (DEPTH, D_MODEL, N_PEER_HEADS * PEER_QUERY_DIM), D_MODEL ** -0.5),
        "sub_keys": nrm(ks[15], (DEPTH, N_PEER_HEADS, 2, N_KEYS, SUBKEY_DIM), SUBKEY_DIM ** -0.5),
        "expert_u": nrm(ks[16], (DEPTH, N_EXPERTS, D_MODEL), D_MODEL ** -0.5),
        "expert_v": nrm(ks[17], (DEPTH, N_EXPERTS, D_MODEL), N_PEER_HEADS ** -0.5),
        "final_norm_w": 1.0 + nrm(ks[18], (D_MODEL,), 0.05),
    }

def first_block(x, c, ada_w, ada_b, norm_mix_w, w_in, q_norm_w, k_norm_w, w_attn_o, pool_mix_w,
              pool_scale, w_pool_o, w_out, norm_ffn_w, w_query, sub_keys, expert_u, expert_v,
              final_norm_w):
    B, S, _ = x.shape
    ang_r, ang_c = axial_rope_angles(S)
    c_act = jax.nn.silu(c)
    splits = [ATTN_WIDTH, ATTN_WIDTH + KV_WIDTH, ATTN_WIDTH + 2 * KV_WIDTH,
              ATTN_WIDTH + 2 * KV_WIDTH + POOL_WIDTH, ATTN_WIDTH + 2 * KV_WIDTH + POOL_WIDTH + D_MODEL]
    for l in range(DEPTH):
        mod = c_act @ ada_w[l] + ada_b[l]
        sh1, sc1, g1, sh2, sc2, g2 = jnp.split(mod, N_ADA, axis=-1)

        xm = modulate(rms_norm(x, norm_mix_w[l]), sh1, sc1)
        proj = xm @ w_in[l]
        q, k, v, u_pool, ga, gp = jnp.split(proj, splits, axis=-1)

        q = rms_norm(q.reshape(B, S, N_HEADS, HEAD_DIM), q_norm_w[l])
        k = rms_norm(k.reshape(B, S, N_KV_HEADS, HEAD_DIM), k_norm_w[l])
        v = v.reshape(B, S, N_KV_HEADS, HEAD_DIM)
        q = apply_axial_rope(q, ang_r, ang_c).reshape(B, S, N_KV_HEADS, GROUP, HEAD_DIM)
        k = apply_axial_rope(k, ang_r, ang_c)
        attn = blocked_bidirectional_gqa(q, k, v) @ w_attn_o[l]

        pool = multiscale_pool(u_pool, pool_mix_w[l], pool_scale[l]) @ w_pool_o[l]

        merged = jax.nn.sigmoid(ga) * attn + jax.nn.sigmoid(gp) * pool
        x = x + g1[:, None, :] * (merged @ w_out[l])

        xf = modulate(rms_norm(x, norm_ffn_w[l]), sh2, sc2)
        x = x + g2[:, None, :] * peer_ffn(xf, w_query[l], sub_keys[l], expert_u[l], expert_v[l])

    return rms_norm(x, final_norm_w)


CTX_LEN = 256
N_HEADS_2 = 16
HEAD_DIM_2 = D_MODEL // N_HEADS_2
D_FF = 2816
N_MIXERS = 2
NA_KH_MAX = 8
NA_KW = 16
NA_QC = 16
NA_KBW = 2 * NA_KW
CONV_W = 3
ROPE_BASE = 10000.0
N_MOD = 9
N_NA_LAYERS = (DEPTH + N_MIXERS - 1) // N_MIXERS
N_CONV_LAYERS = DEPTH // N_MIXERS
DN_ALPHA = (2.0 * DEPTH) ** 0.25
DN_BETA = (8.0 * DEPTH) ** -0.25
LN_EPS = 1e-6


def layer_norm(x, g, b):
    xf = x.astype(jnp.float32)
    mu = jnp.mean(xf, axis=-1, keepdims=True)
    var = jnp.mean(jnp.square(xf - mu), axis=-1, keepdims=True)
    return ((xf - mu) * lax.rsqrt(var + LN_EPS)).astype(x.dtype) * g + b

def modulate_2(x, shift, scale):
    return x * (1 + scale) + shift

def post_norm_update(x, y, gate, res_w, g, b):
    return layer_norm(DN_ALPHA * x + res_w * gate * y, g, b)

def swiglu_ffn(h, w_in, w_out):
    a, u = jnp.split(h @ w_in, 2, axis=-1)
    return (jax.nn.silu(a) * u) @ w_out

def half_step_ffn(x, shift, scale, gate, w_in, w_out, g, b):
    y = swiglu_ffn(modulate_2(x, shift, scale), w_in, w_out)
    return post_norm_update(x, y, gate, 0.5, g, b)

def axial_rope_tables(n_tok):
    t = np.arange(n_tok)
    n_freq = HEAD_DIM_2 // 4
    inv_freq = ROPE_BASE ** (-np.arange(n_freq) / n_freq)
    ang_row = (t // GRID_W)[:, None] * inv_freq[None]
    ang_col = (t % GRID_W)[:, None] * inv_freq[None]
    return (jnp.asarray(np.cos(ang_row), jnp.float32), jnp.asarray(np.sin(ang_row), jnp.float32),
            jnp.asarray(np.cos(ang_col), jnp.float32), jnp.asarray(np.sin(ang_col), jnp.float32))

def _rotate(x, cos, sin):
    x1, x2 = jnp.split(x, 2, axis=-1)
    cos = cos[None, :, None, :].astype(x.dtype)
    sin = sin[None, :, None, :].astype(x.dtype)
    return jnp.concatenate([x1 * cos - x2 * sin, x2 * cos + x1 * sin], axis=-1)

def apply_axial_rope_2(x, tables):
    cos_r, sin_r, cos_c, sin_c = tables
    half = HEAD_DIM_2 // 2
    return jnp.concatenate([_rotate(x[..., :half], cos_r, sin_r),
                            _rotate(x[..., half:], cos_c, sin_c)], axis=-1)

def neighbourhood_attention(hx, hc, w_qkv, w_out, rpb, rope, with_ctx_queries):
    B, S, D = hx.shape
    rows = S // GRID_W
    kh = min(NA_KH_MAX, rows)
    ncb = GRID_W // NA_QC
    nk = kh * NA_KBW
    scale = HEAD_DIM_2 ** -0.5

    qkv = (hx @ w_qkv).reshape(B, S, 3, N_HEADS_2, HEAD_DIM_2)
    q = apply_axial_rope_2(qkv[:, :, 0], rope)
    k = apply_axial_rope_2(qkv[:, :, 1], rope)
    v = qkv[:, :, 2]
    qkv_c = (hc @ w_qkv).reshape(B, hc.shape[1], 3, N_HEADS_2, HEAD_DIM_2)
    q_c, k_c, v_c = qkv_c[:, :, 0], qkv_c[:, :, 1], qkv_c[:, :, 2]

    q_col = np.arange(ncb)[:, None] * NA_QC + np.arange(NA_QC)[None]
    win_c0 = np.clip(q_col - NA_KW // 2, 0, GRID_W - NA_KW)
    blk_c0 = np.clip(np.arange(ncb) * NA_QC - NA_KW // 2, 0, GRID_W - NA_KBW)
    key_col = blk_c0[:, None] + np.arange(NA_KBW)[None]
    col_ok = (key_col[:, None, :] >= win_c0[..., None]) & (key_col[:, None, :] < win_c0[..., None] + NA_KW)
    mask = jnp.asarray(np.broadcast_to(col_ok[:, :, None, :], (ncb, NA_QC, kh, NA_KBW)).reshape(ncb, NA_QC, nk))
    dx_idx = np.clip(key_col[:, None, :] - q_col[..., None] + NA_KW - 1, 0, 2 * NA_KW - 2)
    dx_b = np.broadcast_to(dx_idx[:, :, None, :], (ncb, NA_QC, kh, NA_KBW))

    k_grid = k.reshape(B, rows, GRID_W, N_HEADS_2, HEAD_DIM_2)
    v_grid = v.reshape(B, rows, GRID_W, N_HEADS_2, HEAD_DIM_2)
    q_rows = jnp.moveaxis(q.reshape(B, rows, ncb, NA_QC, N_HEADS_2, HEAD_DIM_2), 1, 0)

    def row_block(args):
        r, q_r = args
        rs = jnp.clip(r - kh // 2, 0, rows - kh)
        k_rows = lax.dynamic_slice_in_dim(k_grid, rs, kh, axis=1)
        v_rows = lax.dynamic_slice_in_dim(v_grid, rs, kh, axis=1)
        k_blk = jnp.moveaxis(k_rows[:, :, key_col], 2, 1).reshape(B, ncb, nk, N_HEADS_2, HEAD_DIM_2)
        v_blk = jnp.moveaxis(v_rows[:, :, key_col], 2, 1).reshape(B, ncb, nk, N_HEADS_2, HEAD_DIM_2)
        dy_idx = rs + jnp.arange(kh) - r + NA_KH_MAX - 1
        bias = rpb[:, dy_idx[None, None, :, None], dx_b].reshape(N_HEADS_2, ncb, NA_QC, nk)
        s_win = jnp.einsum('bjqhd,bjkhd->bhjqk', q_r, k_blk).astype(jnp.float32) * scale
        s_win = jnp.where(mask, s_win + bias.astype(jnp.float32)[None], -jnp.inf)
        s_ctx = jnp.einsum('bjqhd,bchd->bhjqc', q_r, k_c).astype(jnp.float32) * scale
        p = jax.nn.softmax(jnp.concatenate([s_win, s_ctx], axis=-1), axis=-1).astype(v.dtype)
        return (jnp.einsum('bhjqk,bjkhd->bjqhd', p[..., :nk], v_blk)
                + jnp.einsum('bhjqc,bchd->bjqhd', p[..., nk:], v_c))

    o = lax.map(row_block, (jnp.arange(rows), q_rows))
    y_lat = jnp.moveaxis(o, 0, 1).reshape(B, S, D) @ w_out

    y_ctx = None
    if with_ctx_queries:
        s = jnp.einsum('bqhd,bkhd->bhqk', q_c, k_c).astype(jnp.float32) * scale
        p = jax.nn.softmax(s, axis=-1).astype(v_c.dtype)
        y_ctx = jnp.einsum('bhqk,bkhd->bqhd', p, v_c).reshape(B, hc.shape[1], D) @ w_out
    return y_lat, y_ctx

def short_conv_mixer(h, w_in, conv_w, w_out):
    b_gate, c_gate, hv = jnp.split(h @ w_in, 3, axis=-1)
    u = c_gate * hv
    n = u.shape[1]
    pad = CONV_W // 2
    up = jnp.pad(u, ((0, 0), (pad, pad), (0, 0)))
    y = conv_w[0] * up[:, 0:n]
    for j in range(1, CONV_W):
        y = y + conv_w[j] * up[:, j:j + n]
    return (b_gate * y) @ w_out

def second_inputs(seed: int = 0) -> dict:
    key = jax.random.key(seed)
    ks = jax.random.split(key, 16)
    D, F = D_MODEL, D_FF

    def nrm(k, shape, s):
        return jax.random.normal(k, shape, jnp.float32) * s

    return {
        "x": nrm(ks[0], (BATCH, SEQ, D), 1.0),
        "c": nrm(ks[1], (BATCH, D), 1.0),
        "ctx": nrm(ks[2], (BATCH, CTX_LEN, D), 1.0),
        "c_ctx": nrm(ks[3], (D,), 1.0),
        "ada_w": nrm(ks[4], (DEPTH, D, N_MOD * D), 0.5 * D ** -0.5),
        "ada_b": nrm(ks[5], (DEPTH, N_MOD * D), 0.02),
        "ln_g": 1.0 + nrm(ks[6], (DEPTH, 3, D), 0.02),
        "ln_b": nrm(ks[7], (DEPTH, 3, D), 0.02),
        "ffn_w_in": nrm(ks[8], (DEPTH, 2, D, 2 * F), D ** -0.5),
        "ffn_w_out": nrm(ks[9], (DEPTH, 2, F, D), DN_BETA * F ** -0.5),
        "na_w_qkv": nrm(ks[10], (N_NA_LAYERS, D, 3 * D), D ** -0.5),
        "na_w_out": nrm(ks[11], (N_NA_LAYERS, D, D), DN_BETA * D ** -0.5),
        "na_rpb": nrm(ks[12], (N_NA_LAYERS, N_HEADS_2, 2 * NA_KH_MAX - 1, 2 * NA_KW - 1), 0.1),
        "sc_w_in": nrm(ks[13], (N_CONV_LAYERS, D, 3 * D), D ** -0.5),
        "sc_conv": nrm(ks[14], (N_CONV_LAYERS, CONV_W, D), CONV_W ** -0.5),
        "sc_w_out": nrm(ks[15], (N_CONV_LAYERS, D, D), DN_BETA * D ** -0.5),
    }

def second_block(x, c, ctx, c_ctx, ada_w, ada_b, ln_g, ln_b, ffn_w_in, ffn_w_out,
              na_w_qkv, na_w_out, na_rpb, sc_w_in, sc_conv, sc_w_out):
    B, S, D = x.shape
    rope = axial_rope_tables(S)
    last_na = max(range(0, DEPTH, N_MIXERS))
    s_c = jax.nn.silu(c)
    s_cc = jax.nn.silu(c_ctx)
    for i in range(DEPTH):
        ctx_in = i <= last_na
        ctx_out = i < last_na
        j = i // N_MIXERS
        m = (s_c @ ada_w[i] + ada_b[i]).reshape(B, N_MOD, 1, D)
        mc = (s_cc @ ada_w[i] + ada_b[i]).reshape(N_MOD, D)

        x = half_step_ffn(x, m[:, 0], m[:, 1], m[:, 2], ffn_w_in[i, 0], ffn_w_out[i, 0], ln_g[i, 0], ln_b[i, 0])
        if ctx_in:
            ctx = half_step_ffn(ctx, mc[0], mc[1], mc[2], ffn_w_in[i, 0], ffn_w_out[i, 0], ln_g[i, 0], ln_b[i, 0])

        hx = modulate_2(x, m[:, 3], m[:, 4])
        y_ctx = None
        if i % N_MIXERS == 0:
            hc = modulate_2(ctx, mc[3], mc[4])
            y_lat, y_ctx = neighbourhood_attention(hx, hc, na_w_qkv[j], na_w_out[j], na_rpb[j], rope, ctx_out)
        else:
            y_lat = short_conv_mixer(hx, sc_w_in[j], sc_conv[j], sc_w_out[j])
            if ctx_out:
                y_ctx = short_conv_mixer(modulate_2(ctx, mc[3], mc[4]), sc_w_in[j], sc_conv[j], sc_w_out[j])
        x = post_norm_update(x, y_lat, m[:, 5], 1.0, ln_g[i, 1], ln_b[i, 1])
        if ctx_out:
            ctx = post_norm_update(ctx, y_ctx, mc[5], 1.0, ln_g[i, 1], ln_b[i, 1])

        x = half_step_ffn(x, m[:, 6], m[:, 7], m[:, 8], ffn_w_in[i, 1], ffn_w_out[i, 1], ln_g[i, 2], ln_b[i, 2])
        if ctx_out:
            ctx = half_step_ffn(ctx, mc[6], mc[7], mc[8], ffn_w_in[i, 1], ffn_w_out[i, 1], ln_g[i, 2], ln_b[i, 2])
    return x


def setup_inputs(seed=0):
    out = dict(first_inputs(seed))
    for name, value in second_inputs(seed + 1).items():
        if name != "x":
            out[name + "_2"] = value
    return out


def reference(
    x, c, ada_w, ada_b, norm_mix_w, w_in, q_norm_w, k_norm_w, w_attn_o, pool_mix_w, pool_scale,
    w_pool_o, w_out, norm_ffn_w, w_query, sub_keys, expert_u, expert_v, final_norm_w, c_2,
    ctx_2, c_ctx_2, ada_w_2, ada_b_2, ln_g_2, ln_b_2, ffn_w_in_2, ffn_w_out_2, na_w_qkv_2,
    na_w_out_2, na_rpb_2, sc_w_in_2, sc_conv_2, sc_w_out_2,
):
    x = first_block(
        x, c, ada_w, ada_b, norm_mix_w, w_in, q_norm_w, k_norm_w, w_attn_o, pool_mix_w,
        pool_scale, w_pool_o, w_out, norm_ffn_w, w_query, sub_keys, expert_u, expert_v,
        final_norm_w,
    )
    return second_block(
        x, c_2, ctx_2, c_ctx_2, ada_w_2, ada_b_2, ln_g_2, ln_b_2, ffn_w_in_2, ffn_w_out_2,
        na_w_qkv_2, na_w_out_2, na_rpb_2, sc_w_in_2, sc_conv_2, sc_w_out_2,
    )


_drawn_inputs = setup_inputs


def setup_inputs(seed=0):
    import zlib

    import numpy as np

    out = dict(_drawn_inputs(seed))
    spreads = {}
    factors = {'ada_b': 3.935,
     'norm_mix_w': 3.745,
     'q_norm_w': 8.0,
     'k_norm_w': 8.0,
     'pool_scale': 4.09,
     'norm_ffn_w': 2.795,
     'ctx_2': 200.0,
     'ada_b_2': 4.44,
     'na_rpb_2': 64.0,
     'c_ctx_2': 8.0}
    for name, (base, spread) in spreads.items():
        noise = np.random.default_rng([zlib.crc32(name.encode()), seed]).standard_normal(out[name].shape)
        drawn = base * np.exp(spread * noise) if base else spread * noise
        out[name] = jnp.asarray(drawn.astype(out[name].dtype))
    for name, factor in factors.items():
        out[name] = (out[name] * factor).astype(out[name].dtype)
    return out
```

```python
from collections import namedtuple

import numpy as np

import concourse.bass as bass
from concourse import mybir
from concourse.alu_op_type import AluOpType as ALU

F32 = mybir.dt.float32
F32R = mybir.dt.float32r
U32 = mybir.dt.uint32
ACT = mybir.ActivationFunctionType
AX = mybir.AxisListType

P = 128
D = 1024
KT = D // P
T = 256
TT = T // P
DEPTH = 2
GRID_W = 64
EPS = 1e-6
HEADS, KV_HEADS, HEAD_DIM = 8, 2, 128
POOL_GROUPS = 4
POOL_WINDOWS = (2, 4, 8, 16)
W_IN_TILES = 32
PEER_HEADS, TOPK, KEYS = 8, 16, 128
LISTS = 2 * PEER_HEADS
HEADS2, HEAD_DIM2 = 16, 64
FF_TILES = 22
ROWS = T // GRID_W
NA_KW = 16
RPB_H, RPB_W = 15, 31
ALPHA = (2.0 * DEPTH) ** 0.25
MASKED = -1e30

ADA2_GATES = 4
ADA2_CHOICE = (2, 8)
ADA2_FIRST = (0, ADA2_CHOICE[0] + ADA2_GATES)

UNIT = 1024
HALF = UNIT // 2

Stage = namedtuple("Stage", "name units split source q s r g")


def plan():
    rows = []
    sources = {}
    placed = 0

    def add(name, units, split, groups=0, source=None, skip=0):
        nonlocal placed
        if source is None:
            sources[name] = placed
            placed += units
            rows.append((name, units, split, sources[name], groups))
        else:
            rows.append((name, units, split, sources[source] + skip, groups))

    add("ada1.0", 48, False)
    for l in range(DEPTH):
        add(f"w_in.{l}", W_IN_TILES, True, W_IN_TILES)
        add(f"attn_o.{l}", KT, True, KT)
        add(f"pool_mix.{l}", 1, False)
        add(f"pool_o.{l}", POOL_GROUPS, True)
        add(f"w_out.{l}", KT, True, KT)
        add(f"query.{l}", 32, True, 32)
        add(f"sub_keys.{l}", 4, False)
        if l == 0:
            add("ada1.1", 48, False)
        add(f"ada2_choice.{l}", KT * ADA2_CHOICE[l], False)
        add(f"ada2_gates.{l}", KT * ADA2_GATES, False)
        add(f"experts.{l}", 2 * KEYS, True, KEYS)
    add("ffn.0.0", 3 * FF_TILES, True, FF_TILES)
    add("ffn.0.0.x", 3 * FF_TILES, True, FF_TILES, source="ffn.0.0")
    add("qkv", 24, True, 24)
    add("kv_ctx", 16, True, 16, source="qkv", skip=8)
    add("na_o", KT, True, KT)
    add("ffn.0.1", 3 * FF_TILES, True, FF_TILES)
    add("ffn.1.0", 3 * FF_TILES, True, FF_TILES)
    add("conv_in", 24, True, 24)
    add("conv_o", KT, True, KT)
    add("ffn.1.1", 3 * FF_TILES, True, FF_TILES)

    out, q, s, r, g = {}, 0, 0, 0, 0
    for name, units, split, source, groups in rows:
        out[name] = Stage(name, units, split, source, q, s, r, g)
        q += units
        s += units * split
        r += units * (not split)
        g += groups
    return out, placed


COLUMNS = [("c", KT), ("c_2", KT), ("c_ctx", KT), ("final_norm", KT)]
for _l in range(DEPTH):
    COLUMNS += [(f"ada_b.{_l}", 48), (f"norm_mix.{_l}", KT), (f"norm_ffn.{_l}", KT), (f"q_norm.{_l}", 1),
                (f"k_norm.{_l}", 1), (f"pool_scale.{_l}", POOL_GROUPS), (f"ada_b_2.{_l}", 72)]
    for _k in range(3):
        COLUMNS += [(f"ln_g.{_l}.{_k}", KT), (f"ln_b.{_l}.{_k}", KT)]
COLUMNS += [("conv.0", KT), ("conv.1", KT), ("conv.2", KT)]


def column_places():
    at, out = 0, {}
    for name, n in COLUMNS:
        out[name] = (at, n)
        at += n
    return out, at


TABLES = [("ident", P), ("iota", P), ("cos1", T), ("sin1", T), ("swap1", P), ("inv_count", POOL_GROUPS * T),
          ("cos2", T), ("sin2", T), ("swap2", P), ("mask", GRID_W)]


def table_places():
    at, out = 0, {}
    for name, n in TABLES:
        out[name] = (at, n)
        at += n
    return out, at


class Steps:

    def __init__(self):
        self.n = 0

    def one(self):
        self.n += 1
        return 1


class Seen:

    def __init__(self):
        self.at = {}

    def __call__(self, name, k=1):
        self.at[name] = self.at.get(name, 0) + k
        return self.at[name]


def build(nc, ctx, stream, columns, tables, x_in, ctx_in, rpb, out):
    stages, _ = plan()
    col_at, n_cols = column_places()
    tab_at, _ = table_places()

    def sb(name, shape, dt=F32):
        return ctx.enter_context(nc.sbuf_tensor(name, shape, dt))

    def sem(name):
        return ctx.enter_context(nc.semaphore(name))

    X = sb("X", [P, KT, T])
    XH = sb("XH", [P, KT, T], F32R)
    XL = sb("XL", [P, KT, T], F32R)
    raw = sb("raw", [P, 4, UNIT])
    wh = sb("wh", [P, 4, HALF], F32R)
    wl = sb("wl", [P, 4, HALF], F32R)
    AH = sb("AH", [P, 2, T], F32R)
    AL = sb("AL", [P, 2, T], F32R)
    AG = sb("AG", [P, 2, T])
    AP_ = sb("AP_", [P, 2, T])
    arena = sb("arena", [P, T * KEYS])
    cols = sb("cols", [P, n_cols])
    ident = sb("ident", [P, P])
    iota = sb("iota", [P, P])
    mean_d = sb("mean_d", [P, P])
    mean_h = sb("mean_h", [P, P])
    eps = sb("eps", [P, 1])
    cs = sb("cs", [P, 3, KT])
    cs2 = sb("cs2", [P, KT, 2])
    mod1 = sb("mod1", [P, DEPTH, 48])
    mod2 = sb("mod2", [P, DEPTH, 72, 2])
    mod2_flat = mod2[:, :, :, :].rearrange("p l n c -> p (l n c)")
    scale = sb("scale", [P, KT])
    routed = sb("routed", [P, 3, T])
    weight_hi = sb("weight_hi", [P, T], F32R)
    rows = sb("rows", [2, UNIT])
    small = sb("small", [P, 64])
    banks = [ctx.enter_context(nc.psum_tensor(f"bank{i}", [P, 512], F32)) for i in range(8)]

    def A(at, n):
        return arena[:, at:at + n]

    def tiles(at, n, w=T):
        return arena[:, at:at + n * w].rearrange("p (n w) -> p n w", w=w)

    def spread(view, n):
        return view.unsqueeze(1).broadcast_to([P, n, view.shape[-1]])

    def column(name, k=0, n=1):
        at = col_at[name][0]
        return cols[:, at + k:at + k + n]

    gates = arena[:, :].rearrange("p (t j) -> p t j", j=KEYS)

    PROJ, SQ, QW, ROT, ROPED, RMS = 0, 8192, 10752, 13312, 15872, 18432
    VN, PR, PT = 20992, 21504, 22528
    TAB1 = 23552
    PAD, S2, S4, S8, S16, PM = 25216, 26304, 27392, 28208, 28752, 29024
    NORMED, MODUL, ATTNO = 10240, 12288, 8192
    PADW = T + 16
    QUERY, SCORES, REPL, CAND, CREPL, EQ, PICK = 0, 8192, 12288, 14336, 16384, 18432, 20480
    VALS, IDXU, IDXF = 22528, 22784, 23040
    TOPV, TOPU, TOPA, TOPB, TMPU = 23296, 23424, 23552, 23680, 24192
    CHOICES = 24320
    def one_hots(k):
        k = k % 2
        return (wh[:, k, :], (AG, AP_)[k][:, :, :].rearrange("p a w -> p (a w)"), wh[:, 2 + k, :], wl[:, k, :])
    CTX, BIAS, ZC, ZSQ, TAB2 = 0, 2048, 10240, 12288, 14336
    QT, KTL, VT, KTC, VTC, TMP, VNAT = 16384, 18432, 20480, 22528, 24576, 26624, 28672
    PR2, PT2 = 10240, 12288
    CONV, CU, CT = 14336, 2048, 4352

    cos1, sin1 = A(TAB1, T), A(TAB1 + T, T)
    swap1 = A(TAB1 + 2 * T, P)
    inv_count = tiles(TAB1 + 2 * T + P, POOL_GROUPS)
    cos2, sin2 = A(TAB2, T), A(TAB2 + T, T)
    swap2 = A(TAB2 + 2 * T, P)
    mask = A(TAB2 + 2 * T + P, GRID_W)

    raw_ready = [sem(f"raw_ready{i}") for i in range(4)]
    hi_ready = sem("hi_ready")
    lo_ready = sem("lo_ready")
    halves_free = sem("halves_free")
    raw_used = sem("raw_used")
    group_free = sem("group_free")
    prepared = sem("prepared")
    x_loaded = sem("x_loaded")
    tables_loaded = sem("tables_loaded")
    bias_loaded = sem("bias_loaded")
    stored = sem("stored")
    constants_set = sem("constants_set")
    silu_ready = sem("silu_ready")
    rows_copied = sem("rows_copied")
    mod_turned = sem("mod_turned")
    mod_copied = sem("mod_copied")
    mod_ready = sem("mod_ready")
    squares_ready = sem("squares_ready")
    stat_ready = sem("stat_ready")
    rms_ready = sem("rms_ready")
    m_ready = sem("m_ready")
    xh_ready = sem("xh_ready")
    xl_ready = sem("xl_ready")
    centred = sem("centred")
    act_fn = sem("act_fn")
    ah_ready = sem("ah_ready")
    act_ready = sem("act_ready")
    dve_step = sem("dve_step")
    act_step = sem("act_step")
    space_free = sem("space_free")
    x_done = sem("x_done")
    head_squares = sem("head_squares")
    head_sums = sem("head_sums")
    head_rms = sem("head_rms")
    v_transposed = sem("v_transposed")
    v_ready = sem("v_ready")
    weighted = sem("weighted")
    swapped = sem("swapped")
    roped = sem("roped")
    gates_sig = sem("gates_sig")
    scores_ready = sem("scores_ready")
    negmax_ready = sem("negmax_ready")
    exp_done = sem("exp_done")
    probs_ready = sem("probs_ready")
    transposed = sem("transposed")
    pt_copied = sem("pt_copied")
    pv_done = sem("pv_done")
    pool_ready = sem("pool_ready")
    acc_done = sem("acc_done")
    route_scores = sem("route_scores")
    route_evacuated = sem("route_evacuated")
    top_shifted = sem("top_shifted")
    top_exp = sem("top_exp")
    choices_ready = sem("choices_ready")
    choices_turned = sem("choices_turned")
    choices_copied = sem("choices_copied")
    onehots_ready = sem("onehots_ready")
    hot_step = sem("hot_step")
    low_ready = sem("low_ready")
    onehots_free = sem("onehots_free")
    gate_banks_free = sem("gate_banks_free")
    evacuated = sem("evacuated")

    SLOTS = 4
    BATCH = 4
    BATCHES = T // BATCH
    ROUND = BATCHES // ADA2_GATES

    block = ctx.enter_context(nc.Block())

    def mod_places(name):
        return 0 if name.startswith("ada1") else 64

    def pair_steps(nin):
        count = KEYS if nin == 1 else FF_TILES
        body = 2 if nin == 1 else 4
        rounds = (count - 1) // body
        return count, body, rounds

    @block.sync
    def _(sp):
        seen = Seen()

        def released(unit):
            for st in stages.values():
                if st.q <= unit < st.q + st.units:
                    k = unit - st.q
                    return (lo_ready, 2 * (st.s + k) + 2) if st.split else (raw_used, st.r + k + 1)

        sp.dma_start(cols[:, :], columns).then_inc(prepared, 16)
        sp.dma_start(ident[:, :], tables[:, tab_at["ident"][0]:tab_at["ident"][0] + P]).then_inc(prepared, 16)
        sp.dma_start(iota[:, :], tables[:, tab_at["iota"][0]:tab_at["iota"][0] + P]).then_inc(prepared, 16)
        sp.dma_start(X[:, :, :], x_in).then_inc(x_loaded, 16)

        for st in stages.values():
            for k in range(4 if st.units >= 4 else st.units):
                q = st.q + k
                if q >= 4:
                    sp.wait_ge(*released(q - 4))
                sp.dma_start(raw[:, q % 4, :], stream[st.source + k, :, :]).then_inc(raw_ready[q % 4], 16)
            rounds = (st.units - 4) // 4
            if rounds > 0:
                per = 8 if st.split else 4
                with sp.Fori(0, rounds) as i:
                    for b in range(4):
                        q = st.q + 4 + b
                        s, v = released(q - 4)
                        sp.wait_ge(s, v + per * i)
                        sp.dma_start(raw[:, q % 4:q % 4 + 1, :],
                                     stream[bass.ds(st.source + 4 + b + 4 * i, 1), :, :]
                                     .rearrange("a p n -> p a n")).then_inc(raw_ready[q % 4], 16)
            for k in range(4 + 4 * max(rounds, 0), st.units):
                q = st.q + k
                sp.wait_ge(*released(q - 4))
                sp.dma_start(raw[:, q % 4, :], stream[st.source + k, :, :]).then_inc(raw_ready[q % 4], 16)

        sp.wait_ge(x_done, 2 * KT * DEPTH + KT)
        sp.dma_start(out, X[:, :, :]).then_inc(stored, 16)
        sp.wait_ge(stored, 16)

    @block.gpsimd
    def _(pool):
        pool.memset(mean_d[:, :], 1.0 / D).then_inc(constants_set, 1)
        pool.memset(mean_h[:, :], 1.0 / HEAD_DIM).then_inc(constants_set, 1)
        pool.memset(eps[:, :], EPS).then_inc(constants_set, 1)
        at1, _ = tab_at["cos1"]
        at2, _ = tab_at["cos2"]
        for l in range(DEPTH):
            if l:
                pool.wait_ge(space_free, l)
            pool.dma_start(A(TAB1, 2 * T + P + POOL_GROUPS * T),
                           tables[:, at1:at1 + 2 * T + P + POOL_GROUPS * T]).then_inc(tables_loaded, 16)
        pool.wait_ge(space_free, DEPTH)
        pool.dma_start(tiles(CTX, KT), ctx_in).then_inc(tables_loaded, 16)
        pool.dma_start(A(TAB2, 2 * T + P + GRID_W), tables[:, at2:at2 + 2 * T + P + GRID_W]).then_inc(tables_loaded, 16)
        for qb in range(TT):
            for r2 in range(2):
                row = 2 * qb + r2
                dst = arena[64 * r2:64 * r2 + 64, BIAS + qb * HEADS2 * T:BIAS + (qb + 1) * HEADS2 * T]
                pool.dma_start(dst.rearrange("p (h r) -> p h r", h=HEADS2),
                               rpb[:, :, (7 - row) * GRID_W:(7 - row + ROWS) * GRID_W]).then_inc(bias_loaded, 16)

    @block.scalar
    def _(act):
        seen = Seen()
        steps = Steps()
        raws = {}

        def hi(st, k, i=0, per=0):
            s, q = st.s + k, st.q + k
            for half in range(2):
                if half == 0:
                    act.wait_ge(raw_ready[q % 4], 16 * (q // 4 + 1) + 4 * per * i)
                n = 2 * s + half
                act.wait_ge(halves_free, n + 1 + 2 * per * i)
                act.activation(wh[:, n % 4, :], raw[:, q % 4, HALF * half:HALF * (half + 1)],
                               ACT.Copy).then_inc(hi_ready, 1)

        def group_done(st, k, i=0, per=0):
            act.wait_ge(halves_free, SLOTS + 2 * (st.s + k + 1) + 2 * per * i)

        def product(st, evacuate):
            hi(st, 0)
            n = st.units

            def step(k, i, per):
                hi(st, k + 1, i, per)
                if evacuate is not None:
                    group_done(st, k, i, per)
                    evacuate(k + per * i if per else k, banks[4 + (st.g + k) % 2])

            rounds = (n - 1) // 4
            with act.Fori(0, rounds) as i:
                for b in range(4):
                    step(b, i, 4)
            for k in range(4 * rounds, n - 1):
                step(k, 0, 0)
            if evacuate is not None:
                group_done(st, n - 1)
                evacuate(n - 1, banks[4 + (st.g + n - 1) % 2])

        def to_arena(at, func=ACT.Copy, scale=1.0):
            def evacuate(k, bank):
                act.activation(arena[:, bass.ds(at + k * T, T)], bank[:, 0:T], func, scale=scale)\
                   .then_inc(group_free, 1)
            return evacuate

        def pairs(st, nin, func):
            count, body, rounds = pair_steps(nin)
            per = nin + 1

            def first(j, i, body):
                for c in range(nin):
                    hi(st, nin + j * per + c if j >= 0 else c, i, body * per)

            def fn(j, i, body):
                k = nin - 1 if j == 0 and body == 0 else nin + (j - 1) * per + nin - 1
                if j == 0:
                    k = nin - 1 if body == 0 else None
                if k is None:
                    raise AssertionError
                group_done(st, k, i, body * per)
                act.activation(AG[:, j % 2, :], banks[4 + (st.g + j) % 2][:, 0:T], func).then_inc(act_fn, 1)

            def last(j, i, body):
                hi(st, min(nin + j * per + nin, count * per - 1), i, body * per)

            first(-1, 0, 0)
            first(0, 0, 0)
            fn(0, 0, 0)
            last(0, 0, 0)
            loops = (count - 2) // body
            with act.Fori(0, loops) as i:
                for b in range(1, body + 1):
                    first(b, i, body)
                    fn(b, i, body)
                    last(b, i, body)
            for j in range(1 + loops * body, count - 1):
                first(j, 0, 0)
                fn(j, 0, 0)
                last(j, 0, 0)
            fn(count - 1, 0, 0)
            last(count - 1, 0, 0)

        def operand(n, source):
            for k in range(n):
                act.wait_ge(m_ready, seen("m_ready"))
                act.activation(XH[:, k, :], source(k), ACT.Copy).then_inc(xh_ready, 1)

        def rms_stat(src, sq):
            act.activation(sq, src, ACT.Square).then_inc(squares_ready, 1)

        def root(bank, dst):
            act.wait_ge(stat_ready, seen("stat_ready"))
            act.activation(dst, bank, ACT.Sqrt, bias=eps[:, 0:1]).then_inc(rms_ready, 1)

        act.wait_ge(prepared, 48)
        act.wait_ge(constants_set, 3)
        for k, name in enumerate(("c", "c_2", "c_ctx")):
            last = act.activation(cs[:, k, :], column(name, 0, KT), ACT.Silu)
        last.then_inc(act_step, steps.one())
        act.wait_ge(act_step, steps.n)
        act.activation(cs2[:, :, 0], cs[:, 1, :], ACT.Copy)
        act.activation(cs2[:, :, 1], cs[:, 2, :], ACT.Copy).then_inc(silu_ready, 1)

        ada_used = [0]

        def copy_rows(nv, i=0):
            act.wait_ge(raw_used, ada_used[0] + KT + KT * i)
            for half in range(2):
                act.activation(rows[0:nv, HALF * half:HALF * (half + 1)],
                               banks[6 + half][0:nv, :], ACT.Copy).then_inc(rows_copied, 1)

        def ada(name, nv):
            st = stages[name]
            ada_used[0] = st.r
            with act.Fori(0, st.units // KT) as i:
                copy_rows(nv, i)

        def turned(dst, at, n):
            act.wait_ge(mod_turned, seen("mod_turned"))
            act.activation(dst, banks[4][:, at:at + n], ACT.Copy).then_inc(mod_copied, 1)

        rms = A(RMS, T)
        ada("ada1.0", 1)
        turned(mod1[:, 0, :], 0, 48)
        for l in range(DEPTH):
            if l == 0:
                act.wait_ge(x_loaded, 16)
            else:
                act.wait_ge(x_done, seen("x_done", KT))
            rms_stat(X[:, :, :], tiles(SQ, KT))
            root(banks[6][:, 0:T], rms)
            operand(KT, lambda k: tiles(MODUL, KT)[:, k, :])
            product(stages[f"w_in.{l}"], to_arena(PROJ))
            act.wait_ge(group_free, 2 + stages[f"w_in.{l}"].g + W_IN_TILES)
            act.activation(tiles(SQ, 10), tiles(PROJ, 10), ACT.Square).then_inc(head_squares, 1)
            for c in range(5):
                act.wait_ge(head_sums, seen("head_sums"))
                act.activation(A(RMS + 512 * c, 512), banks[(0, 1, 2, 3, 6)[c]][:, :], ACT.Sqrt,
                               bias=eps[:, 0:1]).then_inc(head_rms, 1)
            act.wait_ge(v_transposed, seen("v_transposed"))
            act.activation(A(VN, 512), banks[7][:, :], ACT.Copy).then_inc(v_ready, 1)
            act.activation(A(PROJ + 16 * T, 16 * T), A(PROJ + 16 * T, 16 * T), ACT.Sigmoid).then_inc(gates_sig, 1)

            softmax_scale = float(HEAD_DIM) ** -0.5

            def exps(h):
                hh = l * HEADS + h
                act.wait_ge(negmax_ready, hh + 1)
                for qb in range(TT):
                    if hh >= 2:
                        act.wait_ge(transposed, hh - 1)
                    act.activation(A(PR + (h % 2) * 512 + qb * T, T), banks[h % 2][:, qb * T:(qb + 1) * T], ACT.Exp,
                                   bias=small[:, (h % 2) * 8 + 2 + qb:(h % 2) * 8 + 3 + qb], scale=softmax_scale,
                                   accum_out=small[:, (h % 2) * 8 + 4 + qb:(h % 2) * 8 + 5 + qb]).then_inc(exp_done, 1)

            exps(0)
            exps(1)
            for h in range(HEADS):
                hh = l * HEADS + h
                act.wait_ge(transposed, hh + 1)
                if hh >= 2:
                    act.wait_ge(pv_done, hh - 1)
                act.activation(A(PT + (h % 2) * 512, 512), banks[2 + h % 2][:, :], ACT.Copy).then_inc(pt_copied, 1)
                if h + 2 < HEADS:
                    exps(h + 2)
                act.wait_ge(pv_done, hh + 1)
                act.activation(XH[:, h, :], banks[6 + h % 2][:, 0:T], ACT.Copy).then_inc(xh_ready, 1)
            product(stages[f"attn_o.{l}"], to_arena(ATTNO))
            operand(POOL_GROUPS, lambda k: tiles(MODUL, KT)[:, k, :])
            st = stages[f"pool_o.{l}"]
            for k in range(st.units):
                hi(st, k)
            operand(KT, lambda k: tiles(MODUL, KT)[:, k, :])
            product(stages[f"w_out.{l}"], None)
            act.wait_ge(x_done, seen("x_done", KT))
            rms_stat(X[:, :, :], tiles(SQ, KT))
            root(banks[6][:, 0:T], rms)
            operand(KT, lambda k: tiles(MODUL, KT)[:, k, :])
            product(stages[f"query.{l}"], to_arena(QUERY))
            for c in range(4):
                for tt in range(TT):
                    if tt == 0:
                        act.wait_ge(route_scores, seen("route_scores"))
                    else:
                        act.wait_ge(raw_used, stages[f"sub_keys.{l}"].r + c + 1)
                    act.activation(A(SCORES + tt * LISTS * KEYS + c * 512, 512), banks[6 + tt][:, :],
                                   ACT.Copy).then_inc(route_evacuated, 1)
            if l == 0:
                ada("ada1.1", 1)
                turned(mod1[:, 1, :], 0, 48)
            ada(f"ada2_choice.{l}", 2)
            for tt in range(TT):
                act.wait_ge(top_shifted, seen("top_shifted"))
                w = A(CHOICES + 384 * tt + 256, P)
                act.activation(w, w, ACT.Exp).then_inc(top_exp, 1)
            ada_used[0] = stages[f"ada2_gates.{l}"].r
            first = l * BATCHES

            def lows(k, i=0):
                act.wait_ge(hot_step, first + k + 1 + ROUND * i)
                _, unweighted, _, low = one_hots(k)
                for b in range(BATCH):
                    t = BATCH * (k + ROUND * i) + b
                    last = act.activation(low[:, b * P:(b + 1) * P], unweighted[:, b * P:(b + 1) * P], ACT.Copy,
                                          scale=routed[:, 2, bass.ds(t, 1)])
                last.then_inc(low_ready, 1)

            def spread_gates(k, i=0):
                act.wait_ge(onehots_free, 2 + first + k + 1 + ROUND * i)
                act.activation(arena[:, bass.ds((k + ROUND * i) * BATCH * KEYS, BATCH * KEYS)], banks[k % 2][:, :],
                               ACT.Copy).then_inc(gate_banks_free, 1)
            with act.Fori(0, ADA2_GATES) as i:
                for k in range(ROUND):
                    lows(k, i)
                    if k:
                        spread_gates(k - 1, i)
                spread_gates(ROUND - 1, i)
                copy_rows(2, i)
            turned(mod2_flat[:, 16 * ADA2_FIRST[l]:16 * (ADA2_FIRST[l] + ADA2_CHOICE[l] + ADA2_GATES)],
                   64, 16 * (ADA2_CHOICE[l] + ADA2_GATES))
            pairs(stages[f"experts.{l}"], 1, ACT.Gelu)

        act.wait_ge(x_done, seen("x_done", KT))
        rms_stat(X[:, :, :], tiles(ZSQ, KT))
        root(banks[6][:, 0:T], A(TMP, T))

        def layer_norm():
            seen("stat_ready")
            act.wait_ge(centred, seen("centred"))
            act.activation(tiles(ZSQ, KT), tiles(ZC, KT), ACT.Square).then_inc(squares_ready, 1)
            root(banks[7][:, 0:T], A(TMP, T))

        def ffn(name):
            operand(KT, lambda k: tiles(TMP, KT)[:, k, :])
            pairs(stages[name], 2, ACT.Silu)
            layer_norm()

        ffn("ffn.0.0")
        ffn("ffn.0.0.x")
        operand(KT, lambda k: tiles(TMP, KT)[:, k, :])
        product(stages["qkv"], to_arena(QT))
        operand(KT, lambda k: tiles(TMP, KT)[:, k, :])
        product(stages["kv_ctx"], to_arena(KTC))
        for kt in range(4):
            for c in range(2):
                act.wait_ge(v_transposed, seen("v_transposed"))
                act.activation(A(VNAT + kt * D + c * 512, 512), banks[6 + c][:, :], ACT.Copy).then_inc(v_ready, 1)

        def exps2(h):
            act.wait_ge(negmax_ready, DEPTH * HEADS + h + 1)
            for qb in range(TT):
                if h == 0:
                    act.wait_ge(v_ready, 2 + 8)
                if h >= 1:
                    act.wait_ge(transposed, DEPTH * HEADS + h)
                act.activation(A(PR2 + (h % 2) * 1024 + qb * 512, 512), banks[qb][:, :], ACT.Exp,
                               bias=small[:, (h % 2) * 8 + 2 + qb:(h % 2) * 8 + 3 + qb], scale=1.0,
                               accum_out=small[:, (h % 2) * 8 + 4 + qb:(h % 2) * 8 + 5 + qb]).then_inc(exp_done, 1)

        exps2(0)
        for h in range(HEADS2):
            hh = DEPTH * HEADS + h
            act.wait_ge(transposed, hh + 1)
            if h:
                act.wait_ge(pv_done, hh)
            for qb in range(TT):
                act.activation(A(PT2 + qb * 512, 512), banks[2 + qb][:, :], ACT.Copy).then_inc(pt_copied, 1)
            if h + 1 < HEADS2:
                exps2(h + 1)
            if h % 2:
                act.wait_ge(pv_done, hh + 1)
                act.activation(XH[:, h // 2, :], banks[6 + (h // 2) % 2][:, 0:T], ACT.Copy).then_inc(xh_ready, 1)
        product(stages["na_o"], None)
        layer_norm()
        ffn("ffn.0.1")
        ffn("ffn.1.0")
        operand(KT, lambda k: tiles(TMP, KT)[:, k, :])
        product(stages["conv_in"], to_arena(CONV))
        operand(KT, lambda k: tiles(TMP, KT)[:, k, :])
        product(stages["conv_o"], None)
        layer_norm()
        ffn("ffn.1.1")

    @block.vector
    def _(dve):
        seen = Seen()
        steps = Steps()
        tt_op = dve.tensor_tensor
        MUL, ADD, SUB = ALU.mult, ALU.add, ALU.subtract

        def step(ins):
            ins.then_inc(dve_step, steps.one())

        def settle():
            dve.wait_ge(dve_step, steps.n)

        def lo(st, k, i=0, per=0):
            s, q = st.s + k, st.q + k
            for half in range(2):
                n = 2 * s + half
                dve.wait_ge(hi_ready, n + 1 + 2 * per * i)
                tt_op(wl[:, n % 4, :], raw[:, q % 4, HALF * half:HALF * (half + 1)], wh[:, n % 4, :].bitcast(F32),
                      SUB).then_inc(lo_ready, 1)

        def group_done(st, k, i=0, per=0):
            dve.wait_ge(halves_free, SLOTS + 2 * (st.s + k + 1) + 2 * per * i)

        def product(st, evacuate):
            lo(st, 0)
            n = st.units

            def one(k, i, per):
                lo(st, k + 1, i, per)
                if evacuate is not None:
                    group_done(st, k, i, per)
                    evacuate(k + per * i if per else k, banks[4 + (st.g + k) % 2])

            rounds = (n - 1) // 4
            with dve.Fori(0, rounds) as i:
                for b in range(4):
                    one(b, i, 4)
            for k in range(4 * rounds, n - 1):
                one(k, 0, 0)
            if evacuate is not None:
                group_done(st, n - 1)
                evacuate(n - 1, banks[4 + (st.g + n - 1) % 2])

        def residual(factors):
            def evacuate(k, bank):
                dve.scalar_tensor_tensor(X[:, bass.ds(k, 1), :], bank[:, 0:T].unsqueeze(1), factors(k),
                                         X[:, bass.ds(k, 1), :], MUL, ADD).then_inc(group_free, 1)
            return evacuate

        def pairs(st, nin, combine):
            count, body, _ = pair_steps(nin)
            per = nin + 1

            def first(j, i, body):
                for c in range(nin):
                    lo(st, nin + j * per + c if j >= 0 else c, i, body * per)

            def middle(j, i, body):
                g = st.g + j
                n_act = acts[0] + j
                dve.wait_ge(act_fn, n_act + 1 + body * i)
                combine(j, i, body, banks[4 + g % 2]).then_inc(group_free, 1)
                if j >= 2 or body:
                    k = nin + (j - 2) * per + nin
                    dve.wait_ge(halves_free, SLOTS + 2 * (st.s + k + 1) + 2 * body * per * i)
                dve.wait_ge(group_free, 2 + g + 1 + body * i)
                dve.tensor_copy(AH[:, j % 2, :], AP_[:, j % 2, :]).then_inc(ah_ready, 1)
                dve.wait_ge(ah_ready, n_act + 1 + body * i)
                tt_op(AL[:, j % 2, :], AP_[:, j % 2, :], AH[:, j % 2, :].bitcast(F32), SUB).then_inc(act_ready, 1)

            def last(j, i, body):
                lo(st, min(nin + j * per + nin, count * per - 1), i, body * per)

            first(-1, 0, 0)
            first(0, 0, 0)
            middle(0, 0, 0)
            last(0, 0, 0)
            first(1, 0, 0)
            middle(1, 0, 0)
            last(1, 0, 0)
            loops = (count - 3) // body
            with dve.Fori(0, loops) as i:
                for b in range(2, body + 2):
                    first(b, i, body)
                    middle(b, i, body)
                    last(b, i, body)
            for j in range(2 + loops * body, count - 1):
                first(j, 0, 0)
                middle(j, 0, 0)
                last(j, 0, 0)
            middle(count - 1, 0, 0)
            last(count - 1, 0, 0)
            acts[0] += count

        acts = [0]

        def rest(n, source):
            for k in range(n):
                dve.wait_ge(xh_ready, seen("xh_ready"))
                tt_op(XL[:, k, :], source(k), XH[:, k, :].bitcast(F32), SUB).then_inc(xl_ready, 1)

        def scale_plus_one(dst, src, weight=None):
            step(dve.tensor_scalar(dst, src, 1.0, None, ADD))
            settle()
            if weight is not None:
                step(tt_op(dst, dst, weight, MUL))
                settle()

        def modulate(src, dst, sc, sh, n=KT):
            for k in range(n):
                ins = dve.tensor_scalar(dst[:, k, :], src[:, k, :], sc(k), sh(k) if sh else None, MUL,
                                        *([ADD] if sh else []))
                ins.then_inc(m_ready, 1)
            seen("m_ready", n)
            dve.wait_ge(m_ready, seen.at["m_ready"])
            rest(n, lambda k: dst[:, k, :])

        def over_rms(src, dst, rms):
            dve.wait_ge(rms_ready, seen("rms_ready"))
            step(dve.reciprocal(rms, rms))
            settle()
            step(tt_op(dst, src, spread(rms, KT), MUL))
            settle()

        def add_bias(l, which):
            dve.wait_ge(mod_copied, seen("mod_copied"))
            if which == 1:
                step(tt_op(mod1[:, l, :], mod1[:, l, :], column(f"ada_b.{l}", 0, 48), ADD))
            else:
                b = column(f"ada_b_2.{l}", 0, 72)
                step(tt_op(mod2[:, l, :, :], mod2[:, l, :, :], b.unsqueeze(2).broadcast_to([P, 72, 2]), ADD))
            settle()

        dve.wait_ge(prepared, 48)
        X_ = X[:, :, :]
        for l in range(DEPTH):
            if l == 0:
                add_bias(0, 1)
            shift1, scale1, gate1 = (lambda k, a=a: mod1[:, l, a + k:a + k + 1] for a in (0, 8, 16))
            shift2, _, _ = (lambda k, a=a: mod1[:, l, a + k:a + k + 1] for a in (24, 32, 40))
            normed, modul = tiles(NORMED, KT), tiles(MODUL, KT)
            scale_plus_one(scale[:, :], mod1[:, l, 8:16], column(f"norm_mix.{l}", 0, KT))
            over_rms(X_, normed, A(RMS, T))
            modulate(normed, modul, lambda k: scale[:, k:k + 1], shift1)
            st = stages[f"w_in.{l}"]
            product(st, None)
            dve.wait_ge(group_free, 2 + st.g + W_IN_TILES)
            dve.wait_ge(tables_loaded, 16 * (l + 1))
            dve.tensor_scalar(A(QW, 8 * T), A(PROJ, 8 * T), column(f"q_norm.{l}"), None, MUL).then_inc(weighted, 1)
            dve.tensor_scalar(A(QW + 8 * T, 2 * T), A(PROJ + 8 * T, 2 * T), column(f"k_norm.{l}"), None,
                              MUL).then_inc(weighted, 1)
            pad, s2, s4 = tiles(PAD, 4, PADW), tiles(S2, 4, PADW), tiles(S4, 3, PADW)
            s8, s16, pm = tiles(S8, 2, PADW), tiles(S16, 1, PADW), tiles(PM, 4)
            u = tiles(PROJ + 12 * T, 4)
            step(dve.memset(A(PAD, 4 * PADW), 0.0))
            settle()
            step(dve.tensor_copy(pad[:, :, 8:8 + T], u))
            settle()
            step(tt_op(s2[:, :, 1:PADW], pad[:, :, 0:PADW - 1], pad[:, :, 1:PADW], ADD))
            settle()
            step(tt_op(s4[:, :, 2:PADW - 1], s2[:, 1:4, 1:PADW - 2], s2[:, 1:4, 3:PADW], ADD))
            settle()
            step(tt_op(s8[:, :, 4:PADW - 3], s4[:, 1:3, 2:PADW - 5], s4[:, 1:3, 6:PADW - 1], ADD))
            settle()
            step(tt_op(s16[:, :, 8:8 + T], s8[:, 1:2, 4:4 + T], s8[:, 1:2, 12:12 + T], ADD))
            settle()
            for g, s in enumerate((s2, s4, s8, s16)):
                step(tt_op(pm[:, g, :], s[:, 0, 8:8 + T], inv_count[:, g, :], MUL))
            settle()
            tt_op(pm, pm, u, SUB).then_inc(pool_ready, 1)
            dve.wait_ge(weighted, 2 * (l + 1))
            step(tt_op(tiles(ROT, 10), tiles(QW, 10), spread(cos1, 10), MUL))
            for c in range(5):
                dve.wait_ge(head_rms, seen("head_rms"))
                step(dve.reciprocal(A(RMS + 512 * c, 512), A(RMS + 512 * c, 512)))
            for c in range(5):
                dve.wait_ge(swapped, seen("swapped"))
                step(tt_op(tiles(SQ + 512 * c, 2), banks[(0, 1, 2, 3, 6)[c]][:, :].rearrange("p (n w) -> p n w", w=T),
                           spread(sin1, 2), MUL))
            settle()
            step(tt_op(A(ROT, 2560), A(ROT, 2560), A(SQ, 2560), ADD))
            settle()
            tt_op(A(ROPED, 2560), A(ROT, 2560), A(RMS, 2560), MUL).then_inc(roped, 1)
            dve.wait_ge(gates_sig, l + 1)

            softmax_scale = float(HEAD_DIM) ** -0.5

            def maxes(h):
                hh = l * HEADS + h
                o = (h % 2) * 8
                dve.wait_ge(scores_ready, hh + 1)
                step(dve.reduce_max(small[:, o:o + 2], banks[h % 2][:, :].rearrange("p (q k) -> p q k", q=TT), AX.X))
                settle()
                dve.tensor_scalar(small[:, o + 2:o + 4], small[:, o:o + 2], -softmax_scale, None, MUL)\
                   .then_inc(negmax_ready, 1)

            def normalise(h):
                hh = l * HEADS + h
                o = (h % 2) * 8
                dve.wait_ge(exp_done, 2 * (hh + 1))
                step(dve.reciprocal(small[:, o + 6:o + 8], small[:, o + 4:o + 6]))
                settle()
                for qb in range(TT):
                    p = A(PR + (h % 2) * 512 + qb * T, T)
                    dve.tensor_scalar(p, p, small[:, o + 6 + qb:o + 7 + qb], None, MUL).then_inc(probs_ready, 1)

            maxes(0)
            maxes(1)
            normalise(0)
            for h in range(HEADS):
                if h + 2 < HEADS:
                    maxes(h + 2)
                if h + 1 < HEADS:
                    normalise(h + 1)
                dve.wait_ge(xh_ready, seen("xh_ready"))
                tt_op(XL[:, h, :], banks[6 + h % 2][:, 0:T], XH[:, h, :].bitcast(F32), SUB).then_inc(xl_ready, 1)
            st = stages[f"attn_o.{l}"]
            product(st, None)
            dve.wait_ge(raw_used, stages[f"pool_mix.{l}"].r + 1)
            for g in range(POOL_GROUPS):
                dve.tensor_scalar(modul[:, g, :], banks[6 + g // 2][:, (g % 2) * T:(g % 2 + 1) * T],
                                  column(f"pool_scale.{l}", g), None, MUL).then_inc(m_ready, 1)
            seen("m_ready", POOL_GROUPS)
            dve.wait_ge(m_ready, seen.at["m_ready"])
            rest(POOL_GROUPS, lambda k: modul[:, k, :])
            po = stages[f"pool_o.{l}"]
            for k in range(po.units):
                lo(po, k)
            dve.wait_ge(group_free, 2 + st.g + KT)
            step(tt_op(A(ATTNO, KT * T), A(ATTNO, KT * T), A(PROJ + 16 * T, KT * T), MUL))
            dve.wait_ge(acc_done, seen("acc_done"))
            for b in range(4):
                step(tt_op(A(NORMED + 512 * b, 512), A(PROJ + 24 * T + 512 * b, 512), banks[b][:, :], MUL))
            settle()
            for k in range(KT):
                tt_op(modul[:, k, :], tiles(ATTNO, KT)[:, k, :], normed[:, k, :], ADD).then_inc(m_ready, 1)
            seen("m_ready", KT)
            dve.wait_ge(m_ready, seen.at["m_ready"])
            rest(KT, lambda k: modul[:, k, :])
            product(stages[f"w_out.{l}"], residual(lambda k: mod1[:, l, bass.ds(16 + k, 1)]))
            dve.wait_ge(group_free, 2 + stages[f"w_out.{l}"].g + KT)
            for k in range(KT):
                dve.sem_inc(x_done, 1)
            scale_plus_one(scale[:, :], mod1[:, l, 32:40], column(f"norm_ffn.{l}", 0, KT))
            over_rms(X_, normed, A(RMS, T))
            modulate(normed, modul, lambda k: scale[:, k:k + 1], shift2)
            product(stages[f"query.{l}"], None)

            for tt in range(TT):
                RI, RJ, RW = (CHOICES + 384 * tt + P * n for n in range(3))
                scores = tiles(SCORES + tt * LISTS * KEYS, LISTS, KEYS)
                repl = tiles(REPL, LISTS, KEYS)
                vals, idxf = tiles(VALS, LISTS, TOPK), tiles(IDXF, LISTS, TOPK)
                idxu = A(IDXU, LISTS * TOPK).bitcast(U32).rearrange("p (n w) -> p n w", w=TOPK)
                if tt == 0:
                    dve.wait_ge(route_evacuated, 8 * (l + 1))
                for n in range(LISTS):
                    step(nc.vector.max(vals[:, n, 0:8], scores[:, n, :]))
                settle()
                for n in range(LISTS):
                    step(nc.vector.match_replace(repl[:, n, :], vals[:, n, 0:8], scores[:, n, :], -3e38))
                    step(nc.vector.max_index(idxu[:, n, 0:8], vals[:, n, 0:8], scores[:, n, :]))
                settle()
                for n in range(LISTS):
                    step(nc.vector.max(vals[:, n, 8:16], repl[:, n, :]))
                settle()
                for n in range(LISTS):
                    step(nc.vector.max_index(idxu[:, n, 8:16], vals[:, n, 8:16], repl[:, n, :]))
                settle()
                step(dve.tensor_copy(idxf, idxu))
                cand, crepl = tiles(CAND, PEER_HEADS, 256), tiles(CREPL, PEER_HEADS, 256)
                v4 = A(VALS, LISTS * TOPK).rearrange("p (h two k) -> p h two k", two=2, k=TOPK)
                step(tt_op(A(CAND, 2048).rearrange("p (h a b) -> p h a b", a=TOPK, b=TOPK),
                           v4[:, :, 0, :].unsqueeze(3).broadcast_to([P, PEER_HEADS, TOPK, TOPK]),
                           v4[:, :, 1, :].unsqueeze(2).broadcast_to([P, PEER_HEADS, TOPK, TOPK]), ADD))
                settle()
                topv = tiles(TOPV, PEER_HEADS, TOPK)
                topu = A(TOPU, P).bitcast(U32).rearrange("p (n w) -> p n w", w=TOPK)
                for h in range(PEER_HEADS):
                    step(nc.vector.max(topv[:, h, 0:8], cand[:, h, :]))
                settle()
                for h in range(PEER_HEADS):
                    step(nc.vector.match_replace(crepl[:, h, :], topv[:, h, 0:8], cand[:, h, :], -3e38))
                    step(nc.vector.max_index(topu[:, h, 0:8], topv[:, h, 0:8], cand[:, h, :]))
                settle()
                for h in range(PEER_HEADS):
                    step(nc.vector.max(topv[:, h, 8:16], crepl[:, h, :]))
                settle()
                for h in range(PEER_HEADS):
                    step(nc.vector.max_index(topu[:, h, 8:16], topv[:, h, 8:16], crepl[:, h, :]))
                tt_op(tiles(RW, PEER_HEADS, TOPK), topv, topv[:, :, 0:1].broadcast_to([P, PEER_HEADS, TOPK]),
                      SUB).then_inc(top_shifted, 1)
                settle()
                tmpu = A(TMPU, P).bitcast(U32)
                step(dve.tensor_scalar(tmpu, A(TOPU, P).bitcast(U32), 4, None, ALU.logical_shift_right))
                settle()
                step(dve.tensor_copy(A(TOPA, P), tmpu))
                settle()
                step(dve.tensor_scalar(tmpu, A(TOPU, P).bitcast(U32), 15, None, ALU.bitwise_and))
                settle()
                step(dve.tensor_copy(A(TOPB, P), tmpu))
                settle()
                i4 = A(IDXF, LISTS * TOPK).rearrange("p (h two k) -> p h two k", two=2, k=TOPK)
                eq4 = A(EQ, 2048).rearrange("p (h k a) -> p h k a", k=TOPK, a=TOPK)
                for side, top, dst in ((0, TOPA, RI), (1, TOPB, RJ)):
                    step(tt_op(tiles(EQ, P, TOPK), A(top, P).unsqueeze(2).broadcast_to([P, P, TOPK]),
                               iota[:, 0:TOPK].unsqueeze(1).broadcast_to([P, P, TOPK]), ALU.is_equal))
                    settle()
                    step(tt_op(A(PICK, 2048).rearrange("p (h k a) -> p h k a", k=TOPK, a=TOPK), eq4,
                               i4[:, :, side, :].unsqueeze(2).broadcast_to([P, PEER_HEADS, TOPK, TOPK]), MUL))
                    settle()
                    step(dve.reduce_sum(A(dst, P), tiles(PICK, P, TOPK), AX.X))
            for tt in range(TT):
                dve.wait_ge(top_exp, seen("top_exp"))
                w3 = tiles(CHOICES + 384 * tt + 256, PEER_HEADS, TOPK)
                step(dve.reduce_sum(small[:, 0:PEER_HEADS], w3, AX.X))
                settle()
                step(dve.reciprocal(small[:, 8:8 + PEER_HEADS], small[:, 0:PEER_HEADS]))
                settle()
                tt_op(w3, w3, small[:, 8:16].unsqueeze(2).broadcast_to([P, PEER_HEADS, TOPK]),
                      MUL).then_inc(choices_ready, 1)
                dve.wait_ge(choices_ready, TT * l + tt + 1)
            for tt in range(TT):
                tokens = slice(tt * P, (tt + 1) * P)
                dve.wait_ge(choices_turned, seen("choices_turned"))
                bank = banks[(5, 2)[tt]]
                step(dve.tensor_copy(routed[:, 0:2, tokens], bank[:, 0:2 * P].rearrange("p (n w) -> p n w", w=P)))
                step(dve.tensor_copy(weight_hi[:, tokens], bank[:, 2 * P:3 * P]))
                settle()
                step(tt_op(routed[:, 2, tokens], bank[:, 2 * P:3 * P], weight_hi[:, tokens].bitcast(F32), SUB))
            settle()

            def over_tokens(view, t):
                return view[:, bass.ds(t, BATCH)].unsqueeze(2).broadcast_to([P, BATCH, P])

            def batch(view):
                return view.rearrange("p (t w) -> p t w", w=P)

            first = l * BATCHES
            with dve.Fori(0, BATCHES // 2) as i:
                for k in range(2):
                    t = BATCH * k + 2 * BATCH * i
                    hot_j, unweighted, high, _ = one_hots(k)
                    dve.wait_ge(onehots_free, first + k + 1 + 2 * i)
                    keys = spread(iota[:, :], BATCH)
                    tt_op(batch(unweighted), keys, over_tokens(routed[:, 0, :], t), ALU.is_equal)\
                        .then_inc(hot_step, 1)
                    tt_op(batch(hot_j), keys, over_tokens(routed[:, 1, :], t), ALU.is_equal)
                    dve.wait_ge(hot_step, first + k + 1 + 2 * i)
                    tt_op(batch(high), batch(unweighted), over_tokens(weight_hi[:, :].bitcast(F32), t),
                          MUL).then_inc(onehots_ready, 1)

            def gate(j, i, body, bank):
                return tt_op(AP_[:, j % 2, :].unsqueeze(2), AG[:, j % 2, :].unsqueeze(2),
                             gates[:, :, bass.ds(j + body * i, 1)], MUL)
            st = stages[f"experts.{l}"]
            first_gate = 2 + BATCHES * (l + 1)
            dve.wait_ge(gate_banks_free, first_gate)
            pairs(st, 1, gate)
            dve.wait_ge(acc_done, seen("acc_done"))
            for k in range(KT):
                dve.scalar_tensor_tensor(X[:, k, :], banks[k // 2][:, (k % 2) * T:(k % 2 + 1) * T],
                                         mod1[:, l, 40 + k:41 + k], X[:, k, :], MUL, ADD).then_inc(x_done, 1)
            dve.wait_ge(x_done, 2 * KT * (l + 1))
            dve.sem_inc(space_free, 1)
            if l == 0:
                add_bias(1, 1)
                seen("mod_copied")

        dve.wait_ge(rms_ready, seen("rms_ready"))
        step(dve.reciprocal(A(TMP, T), A(TMP, T)))
        settle()
        step(tt_op(tiles(ZC, KT), X_, spread(A(TMP, T), KT), MUL))
        settle()
        for k in range(KT):
            step(dve.tensor_scalar(X[:, k, :], tiles(ZC, KT)[:, k, :], column("final_norm", k), None, MUL))
        settle()

        ctx_tiles, modul, centre = tiles(CTX, KT), tiles(TMP, KT), tiles(ZC, KT)

        def modulated(view, l, base, side):
            scale_plus_one(scale[:, :], mod2[:, l, base + 8:base + 16, side])
            modulate(view, modul, lambda k: scale[:, k:k + 1], lambda k: mod2[:, l, base + k:base + k + 1, side])

        def post_norm(view, l, which, final=False):
            dve.wait_ge(stat_ready, seen("stat_ready"))
            tt_op(centre, view, spread(banks[6][:, 0:T], KT), SUB).then_inc(centred, 1)
            seen("stat_ready")
            dve.wait_ge(rms_ready, seen("rms_ready"))
            step(dve.reciprocal(A(TMP, T), A(TMP, T)))
            dve.wait_ge(centred, seen("centred"))
            settle()
            step(tt_op(centre, centre, spread(A(TMP, T), KT), MUL))
            settle()
            for k in range(KT):
                ins = dve.tensor_scalar(view[:, k, :], centre[:, k, :], column(f"ln_g.{l}.{which}", k),
                                        column(f"ln_b.{l}.{which}", k), MUL, ADD)
                if final:
                    ins.then_inc(x_done, 1)
                else:
                    step(ins)
            settle()

        def post_scale(view, l, base, side, factor):
            step(dve.tensor_scalar(scale[:, :], mod2[:, l, base + 16:base + 24, side], factor, None, MUL))
            step(dve.tensor_scalar(view, view, ALPHA, None, MUL))
            settle()

        def ffn(name, view, l, which, side, final=False):
            base = 0 if which == 0 else 48
            modulated(view, l, base, side)

            def combine(j, i, body, bank):
                return tt_op(AP_[:, j % 2, :], AG[:, j % 2, :], bank[:, T:2 * T], MUL)
            pairs(stages[name], 2, combine)
            post_scale(view, l, base, side, 0.5)
            dve.wait_ge(acc_done, seen("acc_done"))
            for k in range(KT):
                dve.scalar_tensor_tensor(view[:, k, :], banks[k // 2][:, (k % 2) * T:(k % 2 + 1) * T],
                                         scale[:, k:k + 1], view[:, k, :], MUL, ADD).then_inc(evacuated, 1)
            seen("evacuated", KT)
            dve.wait_ge(evacuated, seen.at["evacuated"])
            post_norm(view, l, which, final)

        dve.wait_ge(tables_loaded, 64)
        for l in range(DEPTH):
            if l:
                seen("mod_copied", -1)
            add_bias(l, 2)
        seen("stat_ready", 2 * DEPTH + 1)
        ffn("ffn.0.0", ctx_tiles, 0, 0, 1)
        ffn("ffn.0.0.x", X_, 0, 0, 0)
        modulated(X_, 0, 24, 0)
        product(stages["qkv"], None)
        modulated(ctx_tiles, 0, 24, 1)
        product(stages["kv_ctx"], None)
        st = stages["kv_ctx"]
        for side, at in ((0, QT), (1, KTL)):
            step(tt_op(tiles(TMP, KT), tiles(at, KT), spread(cos2, KT), MUL))
            for c in range(4):
                dve.wait_ge(swapped, seen("swapped"))
                step(tt_op(tiles(PR2 + 512 * c, 2), banks[c][:, :].rearrange("p (n w) -> p n w", w=T),
                           spread(sin2, 2), MUL))
            settle()
            tt_op(A(at, KT * T), A(TMP, KT * T), A(PR2, KT * T), ADD).then_inc(roped, 1)
            dve.wait_ge(roped, 2 + side + 1)
        dve.wait_ge(bias_loaded, 16 * TT * 2)
        both = A(BIAS, TT * HEADS2 * T).rearrange("p (n c) -> p n c", c=GRID_W)
        step(tt_op(both, both, spread(mask, TT * HEADS2 * ROWS), ADD))
        settle()

        def maxes2(h):
            o = (h % 2) * 8
            for qb in range(TT):
                dve.wait_ge(scores_ready, DEPTH * HEADS + 2 * h + qb + 1)
                bias = A(BIAS + (qb * HEADS2 + h) * T, T)
                step(dve.scalar_tensor_tensor(banks[qb][:, 0:T], banks[qb][:, 0:T], float(HEAD_DIM2) ** -0.5, bias,
                                              MUL, ADD))
                step(dve.tensor_scalar(banks[qb][:, T:2 * T], banks[qb][:, T:2 * T], float(HEAD_DIM2) ** -0.5, None,
                                       MUL))
                settle()
                step(dve.reduce_max(small[:, o + qb:o + qb + 1], banks[qb][:, :], AX.X))
            settle()
            dve.tensor_scalar(small[:, o + 2:o + 4], small[:, o:o + 2], -1.0, None, MUL).then_inc(negmax_ready, 1)

        def normalise2(h):
            o = (h % 2) * 8
            dve.wait_ge(exp_done, 2 * (DEPTH * HEADS + h + 1))
            step(dve.reciprocal(small[:, o + 6:o + 8], small[:, o + 4:o + 6]))
            settle()
            for qb in range(TT):
                p = A(PR2 + (h % 2) * 1024 + qb * 512, 512)
                dve.tensor_scalar(p, p, small[:, o + 6 + qb:o + 7 + qb], None, MUL).then_inc(probs_ready, 1)

        maxes2(0)
        normalise2(0)
        for h in range(HEADS2):
            if h + 1 < HEADS2:
                maxes2(h + 1)
                normalise2(h + 1)
            if h % 2:
                dve.wait_ge(xh_ready, seen("xh_ready"))
                tt_op(XL[:, h // 2, :], banks[6 + (h // 2) % 2][:, 0:T], XH[:, h // 2, :].bitcast(F32),
                      SUB).then_inc(xl_ready, 1)
        post_scale(X_, 0, 24, 0, 1.0)
        product(stages["na_o"], residual(lambda k: scale[:, bass.ds(k, 1)]))
        dve.wait_ge(group_free, 2 + stages["na_o"].g + KT)
        dve.sem_inc(evacuated, KT)
        seen("evacuated", KT)
        post_norm(X_, 0, 1)
        ffn("ffn.0.1", X_, 0, 2, 0)
        ffn("ffn.1.0", X_, 1, 0, 0)
        modulated(X_, 1, 24, 0)
        st = stages["conv_in"]
        product(st, None)
        dve.wait_ge(group_free, 2 + st.g + 24)
        cu = tiles(CU, KT, T + 2)
        b_gate, c_gate, hv = tiles(CONV, KT), tiles(CONV + 8 * T, KT), tiles(CONV + 16 * T, KT)
        step(dve.memset(A(CU, KT * (T + 2)), 0.0))
        settle()
        step(tt_op(cu[:, :, 1:1 + T], c_gate, hv, MUL))
        settle()
        conv = tiles(CT, KT)
        for k in range(KT):
            step(dve.tensor_scalar(conv[:, k, :], cu[:, k, 0:T], column("conv.0", k), None, MUL))
        settle()
        for tap in (1, 2):
            for k in range(KT):
                step(dve.scalar_tensor_tensor(conv[:, k, :], cu[:, k, tap:tap + T], column(f"conv.{tap}", k),
                                              conv[:, k, :], MUL, ADD))
            settle()
        for k in range(KT):
            tt_op(modul[:, k, :], conv[:, k, :], b_gate[:, k, :], MUL).then_inc(m_ready, 1)
        seen("m_ready", KT)
        dve.wait_ge(m_ready, seen.at["m_ready"])
        rest(KT, lambda k: modul[:, k, :])
        post_scale(X_, 1, 24, 0, 1.0)
        product(stages["conv_o"], residual(lambda k: scale[:, bass.ds(k, 1)]))
        dve.wait_ge(group_free, 2 + stages["conv_o"].g + KT)
        dve.sem_inc(evacuated, KT)
        seen("evacuated", KT)
        post_norm(X_, 1, 1)
        ffn("ffn.1.1", X_, 1, 2, 0, final=True)

    @block.tensor
    def _(pe):
        seen = Seen()
        acts = [0]
        pe.sem_inc(halves_free, SLOTS)
        pe.sem_inc(onehots_free, 2)
        pe.sem_inc(group_free, 2)
        pe.sem_inc(gate_banks_free, 2)

        def three(out, n, a, b, moving_h, moving_l, start, stop, check=False):
            pe.matmul(out, wh[:, n % 4, a:b], moving_h, start=start, stop=False, skip_group_check=check)
            pe.matmul(out, wh[:, n % 4, a:b], moving_l, start=False, stop=False, skip_group_check=check)
            return pe.matmul(out, wl[:, n % 4, a:b], moving_h, start=False, stop=stop, skip_group_check=check)

        def tile(st, k, i, per, out):
            for half in range(2):
                n = 2 * (st.s + k) + half
                pe.wait_ge(lo_ready, n + 1 + 2 * per * i)
                for kk in range(4):
                    kt = 4 * half + kk
                    last = three(out, n, P * kk, P * (kk + 1), XH[:, kt, :], XL[:, kt, :], kt == 0, kt == KT - 1)
                last.then_inc(halves_free, 1)

        def product(st):
            pe.wait_ge(xl_ready, seen("xl_ready", KT))
            with pe.Fori(0, st.units // 4) as i:
                for b in range(4):
                    pe.wait_ge(group_free, st.g + b + 1 + 4 * i)
                    tile(st, b, i, 4, banks[4 + (st.g + b) % 2][:, 0:T])

        def outer(st, k, i, per, moving_h, moving_l, first, final):
            for half in range(2):
                n = 2 * (st.s + k) + half
                pe.wait_ge(lo_ready, n + 1 + 2 * per * i)
                for kk in range(4):
                    o = 4 * half + kk
                    last = three(banks[o // 2][:, (o % 2) * T:(o % 2 + 1) * T], n, P * kk, P * (kk + 1), moving_h,
                                 moving_l, first and o % 2 == 0, final and o % 2 == 1, True)
                last.then_inc(halves_free, 1)

        def pairs(st, nin):
            count, body, _ = pair_steps(nin)
            per = nin + 1
            if nin == 2:
                pe.wait_ge(xl_ready, seen("xl_ready", KT))

            def first(j, i, body):
                g = st.g + j + 1
                pe.wait_ge(group_free, g + 1 + body * i)
                for c in range(nin):
                    tile(st, nin + j * per + c if j >= 0 else c, i, body * per, banks[4 + g % 2][:, c * T:(c + 1) * T])

            def last(j, i, body, start=False, final=False):
                pe.wait_ge(act_ready, acts[0] + j + 1 + body * i)
                outer(st, min(nin + j * per + nin, count * per - 1), i, body * per, AH[:, j % 2, :], AL[:, j % 2, :], start, final)

            first(-1, 0, 0)
            first(0, 0, 0)
            last(0, 0, 0, start=True)
            loops = (count - 2) // body
            with pe.Fori(0, loops) as i:
                for b in range(1, body + 1):
                    first(b, i, body)
                    last(b, i, body)
            for j in range(1 + loops * body, count - 1):
                first(j, 0, 0)
                last(j, 0, 0)
            last(count - 1, 0, 0, final=True)
            acts[0] += count

        def finish_acc():
            pe.drain().then_inc(acc_done, 1)

        def column_mean(matrix, src, bank, sem_=None):
            for k in range(KT):
                last = pe.matmul(bank[:, 0:T], matrix[:, :], src(k), start=k == 0, stop=k == KT - 1)
            last.then_inc(stat_ready, 1)

        blocks = [0]

        def rows_times(st, vectors, nv, kts, i=0, halves=(0, 1)):
            for kt in kts:
                q = st.q + kt
                if halves[0] == 0:
                    pe.wait_ge(raw_ready[q % 4], 16 * (q // 4 + 1) + 32 * i)
                for half in halves:
                    last = pe.matmul(banks[6 + half][0:nv, :], vectors(kt),
                                     raw[:, q % 4, HALF * half:HALF * (half + 1)],
                                     start=kt == 0, stop=kt == KT - 1)
                if halves[-1] == 1:
                    last.then_inc(raw_used, 1)

        def rows_read(i=0):
            pe.wait_ge(rows_copied, 2 * blocks[0] + 2 * i)

        def turn(at, nv, i=0):
            for f in range(KT):
                at_f = at + nv * f + nv * KT * i
                columns_ = banks[4][:, at_f:at_f + nv] if isinstance(at_f, int) else banks[4][:, bass.ds(at_f, nv)]
                last = pe.matmul(columns_, rows[0:nv, f * P:(f + 1) * P], ident[0:nv, 0:nv],
                                 start=True, stop=True)
            return last

        def ada(name, vectors, nv, at, finish=True):
            st = stages[name]
            n = st.units // KT
            if blocks[0]:
                rows_read()
            rows_times(st, vectors, nv, range(KT))
            with pe.Fori(1, n) as i:
                rows_read(i)
                rows_times(st, vectors, nv, range(4), i)
                turn(at - nv * KT, nv, i)
                rows_times(st, vectors, nv, range(4, KT), i)
            blocks[0] += n
            if finish:
                rows_read()
                turn(at + nv * KT * (n - 1), nv).then_inc(mod_turned, 1)

        def rms_norm(sq):
            pe.wait_ge(squares_ready, seen("squares_ready"))
            column_mean(mean_d, lambda k: tiles(sq, KT)[:, k, :], banks[6])

        pe.wait_ge(silu_ready, 1)
        ada("ada1.0", lambda kt: cs[:, 0, kt:kt + 1], 1, 0)
        pe.wait_ge(mod_copied, seen("mod_copied"))
        for l in range(DEPTH):
            rms_norm(SQ)
            product(stages[f"w_in.{l}"])
            pe.wait_ge(head_squares, l + 1)
            for c in range(5):
                pe.matmul(banks[(0, 1, 2, 3, 6)[c]][:, :], mean_h[:, :], A(SQ + 512 * c, 512), start=True,
                          stop=True).then_inc(head_sums, 1)
            for g in range(KV_HEADS):
                for kt in range(TT):
                    last = pe.transpose(banks[7][:, (g * 2 + kt) * P:(g * 2 + kt + 1) * P],
                                        A(PROJ + (10 + g) * T + kt * P, P), ident[:, :])
            last.then_inc(v_transposed, 1)
            pe.wait_ge(weighted, 2 * (l + 1))
            for c in range(5):
                pe.wait_ge(head_rms, seen("head_rms"))
                pe.matmul(banks[(0, 1, 2, 3, 6)[c]][:, :], swap1, A(QW + 512 * c, 512), start=True,
                          stop=True).then_inc(swapped, 1)

            def scores(h):
                hh = l * HEADS + h
                if h >= 2:
                    pe.wait_ge(exp_done, 2 * (hh - 1))
                for qb in range(TT):
                    last = pe.matmul(banks[h % 2][:, qb * T:(qb + 1) * T], A(ROPED + h * T + qb * P, P),
                                     A(ROPED + (8 + h // 4) * T, T), start=True, stop=True)
                last.then_inc(scores_ready, 1)

            pe.wait_ge(roped, l + 1)
            pe.wait_ge(v_ready, l + 1)
            scores(0)
            scores(1)
            for h in range(HEADS):
                hh = l * HEADS + h
                pe.wait_ge(probs_ready, 2 * (hh + 1))
                if h >= 2:
                    pe.wait_ge(pt_copied, hh - 1)
                for qb in range(TT):
                    for kt in range(TT):
                        last = pe.transpose(banks[2 + h % 2][:, kt * T + qb * P:kt * T + (qb + 1) * P],
                                            A(PR + (h % 2) * 512 + qb * T + kt * P, P), ident[:, :])
                last.then_inc(transposed, 1)
                if h + 2 < HEADS:
                    scores(h + 2)
                pe.wait_ge(pt_copied, hh + 1)
                if h >= 2:
                    pe.wait_ge(xl_ready, seen.at["xl_ready"] + h - 1)
                for kt in range(TT):
                    last = pe.matmul(banks[6 + h % 2][:, 0:T], A(VN + (h // 4) * T + kt * P, P),
                                     A(PT + (h % 2) * 512 + kt * T, T), start=kt == 0, stop=kt == TT - 1)
                last.then_inc(pv_done, 1)
            product(stages[f"attn_o.{l}"])
            st = stages[f"pool_mix.{l}"]
            pe.wait_ge(raw_ready[st.q % 4], 16 * (st.q // 4 + 1))
            pe.wait_ge(pool_ready, l + 1)
            for g in range(POOL_GROUPS):
                last = pe.matmul(banks[6 + g // 2][:, (g % 2) * T:(g % 2 + 1) * T], raw[:, st.q % 4, g * P:(g + 1) * P],
                                 A(PM + g * T, T), start=True, stop=True)
            last.then_inc(raw_used, 1)
            st = stages[f"pool_o.{l}"]
            pe.wait_ge(xl_ready, seen("xl_ready", POOL_GROUPS))
            for k in range(POOL_GROUPS):
                outer(st, k, 0, 0, XH[:, k, :], XL[:, k, :], k == 0, k == POOL_GROUPS - 1)
            finish_acc()
            product(stages[f"w_out.{l}"])
            rms_norm(SQ)
            product(stages[f"query.{l}"])
            st = stages[f"sub_keys.{l}"]
            pe.wait_ge(group_free, 2 + stages[f"query.{l}"].g + 32)
            for c in range(4):
                q = st.q + c
                pe.wait_ge(raw_ready[q % 4], 16 * (q // 4 + 1))
                for tt in range(TT):
                    if c:
                        pe.wait_ge(route_evacuated, 8 * l + 2 * (c - 1) + tt + 1)
                    for n in range(4):
                        for dt in range(2):
                            last = pe.matmul(banks[6 + tt][:, n * P:(n + 1) * P],
                                             A(QUERY + (2 * (4 * c + n) + dt) * T + tt * P, P),
                                             raw[:, q % 4, (2 * n + dt) * P:(2 * n + dt + 1) * P],
                                             start=dt == 0, stop=dt == 1)
                    last.then_inc(route_scores if tt == 0 else raw_used, 1)
            pe.wait_ge(route_evacuated, 8 * (l + 1))
            if l == 0:
                ada("ada1.1", lambda kt: cs[:, 0, kt:kt + 1], 1, 0)
            ada(f"ada2_choice.{l}", lambda kt: cs2[:, kt, :], 2, 64, finish=False)
            for tt in range(TT):
                pe.wait_ge(choices_ready, seen("choices_ready"))
                for n in range(3):
                    last = pe.transpose(banks[(5, 2)[tt]][:, n * P:(n + 1) * P], A(CHOICES + 384 * tt + n * P, P),
                                        ident[:, :])
                last.then_inc(choices_turned, 1)
            st = stages[f"ada2_gates.{l}"]
            first = l * BATCHES
            with pe.Fori(0, ADA2_GATES) as i:
                for k in range(ROUND):
                    hot_j, _, high, low = one_hots(k)
                    pe.wait_ge(gate_banks_free, first + k + 1 + ROUND * i)
                    pe.wait_ge(onehots_ready, first + k + 1 + ROUND * i)
                    pe.wait_ge(low_ready, first + k + 1 + ROUND * i)
                    for b in range(BATCH):
                        at = slice(b * P, (b + 1) * P)
                        pe.matmul(banks[k % 2][:, at], high[:, at], hot_j[:, at], start=True, stop=False)
                        last = pe.matmul(banks[k % 2][:, at], low[:, at], hot_j[:, at], start=False, stop=True)
                    last.then_inc(onehots_free, 1)
                    if k == 0:
                        rows_read(i)
                    rows_times(st, lambda kt: cs2[:, kt, :], 2, (k // 2,), i, (k % 2,))
                    if k == ROUND // 2 - 1:
                        turn(64 + 16 * (ADA2_CHOICE[l] - 1), 2, i)
            blocks[0] += ADA2_GATES
            rows_read()
            turn(64 + 16 * (ADA2_CHOICE[l] + ADA2_GATES - 1), 2).then_inc(mod_turned, 1)
            pe.wait_ge(mod_copied, seen("mod_copied", 2 if l == 0 else 1))
            pairs(stages[f"experts.{l}"], 1)
            finish_acc()
        pe.wait_ge(squares_ready, seen("squares_ready"))
        column_mean(mean_d, lambda k: tiles(ZSQ, KT)[:, k, :], banks[6])

        def post_norm(view):
            pe.wait_ge(evacuated, seen("evacuated", KT))
            column_mean(mean_d, lambda k: view[:, k, :], banks[6])
            pe.wait_ge(squares_ready, seen("squares_ready"))
            column_mean(mean_d, lambda k: tiles(ZSQ, KT)[:, k, :], banks[7])

        def ffn(name, view):
            pairs(stages[name], 2)
            finish_acc()
            post_norm(view)

        ctx_tiles, X_ = tiles(CTX, KT), X[:, :, :]
        ffn("ffn.0.0", ctx_tiles)
        ffn("ffn.0.0.x", X_)
        product(stages["qkv"])
        product(stages["kv_ctx"])
        st = stages["kv_ctx"]
        pe.wait_ge(group_free, 2 + st.g + 16)
        for side, at in ((0, QT), (1, KTL)):
            if side:
                pe.wait_ge(roped, 2 + 1)
            for c in range(4):
                pe.matmul(banks[c][:, :], swap2, A(at + 512 * c, 512), start=True, stop=True).then_inc(swapped, 1)
        for kt in range(4):
            src = VT if kt < 2 else VTC
            for c in range(2):
                if kt:
                    pe.wait_ge(v_ready, 2 + 2 * (kt - 1) + c + 1)
                for f in range(4):
                    last = pe.transpose(banks[6 + c][:, f * P:(f + 1) * P],
                                        A(src + (4 * c + f) * T + (kt % 2) * P, P), ident[:, :])
                last.then_inc(v_transposed, 1)

        def scores2(h):
            hh = DEPTH * HEADS + h
            part = slice(64 * (h % 2), 64 * (h % 2) + 64)
            for qb in range(TT):
                if h:
                    pe.wait_ge(exp_done, 2 * hh - 1 + qb)
                at = (h // 2) * T
                q = arena[part, QT + at + qb * P:QT + at + (qb + 1) * P]
                pe.matmul(banks[qb][:, 0:T], q, arena[part, KTL + at:KTL + at + T], start=True, stop=True)
                pe.matmul(banks[qb][:, T:2 * T], q, arena[part, KTC + at:KTC + at + T], start=True,
                          stop=True).then_inc(scores_ready, 1)

        pe.wait_ge(roped, 2 + 2)
        pe.wait_ge(v_ready, 2 + 8)
        scores2(0)
        for h in range(HEADS2):
            hh = DEPTH * HEADS + h
            for qb in range(TT):
                pe.wait_ge(probs_ready, 2 * hh + qb + 1)
                if h:
                    pe.wait_ge(pt_copied, 2 * 8 + 2 * h)
                for kt in range(4):
                    last = pe.transpose(banks[2 + qb][:, kt * P:(kt + 1) * P],
                                        A(PR2 + (h % 2) * 1024 + qb * 512 + kt * P, P), ident[:, :])
            last.then_inc(transposed, 1)
            if h + 1 < HEADS2:
                scores2(h + 1)
            part = slice(64 * (h % 2), 64 * (h % 2) + 64)
            if h % 2 == 0 and h >= 4:
                pe.wait_ge(xl_ready, seen.at["xl_ready"] + (h - 4) // 2 + 1)
            for qb in range(TT):
                pe.wait_ge(pt_copied, 2 * 8 + 2 * h + qb + 1)
                for kt in range(4):
                    last = pe.matmul(banks[6 + (h // 2) % 2][part, qb * P:(qb + 1) * P],
                                     A(VNAT + kt * D + h * HEAD_DIM2, HEAD_DIM2),
                                     A(PT2 + qb * 512 + kt * P, P), start=kt == 0, stop=kt == 3)
            last.then_inc(pv_done, 1)
        product(stages["na_o"])
        post_norm(X_)
        ffn("ffn.0.1", X_)
        ffn("ffn.1.0", X_)
        product(stages["conv_in"])
        product(stages["conv_o"])
        post_norm(X_)
        ffn("ffn.1.1", X_)


def shape_tables():
    at, n = table_places()
    out = np.zeros((P, n), np.float32)

    def put(name, value):
        a, w = at[name]
        out[:, a:a + w] = value

    put("ident", np.eye(P, dtype=np.float32))
    put("iota", np.arange(P, dtype=np.float32)[None])
    t = np.arange(T)
    row, col = (t // GRID_W).astype(np.float32), (t % GRID_W).astype(np.float32)

    def rope(prefix, head, inv):
        quarter = head // 4
        d = np.arange(P) % head
        half = d // (2 * quarter)
        freq = inv[d % quarter]
        ang = np.where(half[:, None] == 0, row[None], col[None]).astype(freq.dtype) * freq[:, None]
        second = (d // quarter) % 2
        put(f"cos{prefix}", np.cos(ang))
        put(f"sin{prefix}", np.sin(ang) * np.where(second == 1, 1.0, -1.0)[:, None].astype(ang.dtype))
        partner = np.arange(P) + np.where(second == 1, -quarter, quarter)
        swap = np.zeros((P, P), np.float32)
        swap[partner, np.arange(P)] = 1.0
        put(f"swap{prefix}", swap)

    inv1 = (1.0 / (np.float32(10000.0) ** (np.arange(0, 64, 2, dtype=np.float32) / np.float32(64)))).astype(np.float32)
    rope("1", HEAD_DIM, inv1)
    rope("2", HEAD_DIM2, 10000.0 ** (-np.arange(16) / 16))
    counts = [np.clip(t + w // 2, 0, T) - np.clip(t - w // 2, 0, T) for w in POOL_WINDOWS]
    put("inv_count", np.concatenate([1.0 / c for c in counts])[None])
    qc, kc = np.arange(GRID_W)[:, None], np.arange(GRID_W)[None]
    first = np.clip(qc - NA_KW // 2, 0, GRID_W - NA_KW)
    ok = (kc >= first) & (kc < first + NA_KW)
    put("mask", np.tile(np.where(ok, 0.0, MASKED), (2, 1)))
    return out


def tile_units(w):
    n = w.shape[1] // P
    return w.reshape(KT, P, n, P).transpose(2, 1, 0, 3).reshape(n, P, UNIT)


def row_units(w):
    return w.reshape(KT, P, -1, UNIT).transpose(2, 0, 1, 3).reshape(-1, P, UNIT)


def fill_stream(i):
    stages, placed = plan()
    stream = np.empty((placed, P, UNIT), np.float32)

    def put(name, units):
        at = stages[name].source
        stream[at:at + len(units)] = units

    for l in range(DEPTH):
        put(f"ada1.{l}", row_units(i["ada_w"][l]))
        put(f"w_in.{l}", tile_units(i["w_in"][l]))
        put(f"attn_o.{l}", tile_units(i["w_attn_o"][l]))
        mix = np.zeros((1, P, UNIT), np.float32)
        mix[0, :, :POOL_GROUPS * P] = i["pool_mix_w"][l].transpose(1, 0, 2).reshape(P, -1)
        put(f"pool_mix.{l}", mix)
        put(f"pool_o.{l}", i["w_pool_o"][l].reshape(POOL_GROUPS, P, UNIT))
        put(f"w_out.{l}", tile_units(i["w_out"][l]))
        put(f"query.{l}", tile_units(i["w_query"][l]))
        put(f"sub_keys.{l}", i["sub_keys"][l].reshape(4, 4, KEYS, 2, P).transpose(0, 4, 1, 3, 2).reshape(4, P, UNIT))
        at = stages[f"experts.{l}"].source
        u = i["expert_u"][l].reshape(KEYS, KEYS, KT, P).transpose(1, 3, 2, 0).reshape(KEYS, P, UNIT)
        v = i["expert_v"][l].reshape(KEYS, KEYS, UNIT).transpose(1, 0, 2)
        j = np.arange(KEYS)
        stream[at + np.where(j == 0, 0, 2 * j - 1)] = u
        stream[at + np.where(j == KEYS - 1, 2 * KEYS - 1, 2 * j + 2)] = v
        for k in range(2):
            at = stages[f"ffn.{l}.{k}"].source
            w = tile_units(i["ffn_w_in_2"][l, k])
            f = np.arange(FF_TILES)
            first = np.where(f == 0, 0, 3 * f - 1)
            stream[at + first] = w[:FF_TILES]
            stream[at + first + 1] = w[FF_TILES:]
            stream[at + np.where(f == FF_TILES - 1, 3 * FF_TILES - 1, 3 * f + 4)] = \
                i["ffn_w_out_2"][l, k].reshape(FF_TILES, P, UNIT)
    ada2 = np.concatenate([row_units(i["ada_w_2"][l]) for l in range(DEPTH)])
    for l in range(DEPTH):
        first = KT * ADA2_FIRST[l]
        middle, end = first + KT * ADA2_CHOICE[l], first + KT * (ADA2_CHOICE[l] + ADA2_GATES)
        put(f"ada2_choice.{l}", ada2[first:middle])
        put(f"ada2_gates.{l}", ada2[middle:end])
    put("qkv", tile_units(i["na_w_qkv_2"][0]))
    put("na_o", tile_units(i["na_w_out_2"][0]))
    put("conv_in", tile_units(i["sc_w_in_2"][0]))
    put("conv_o", tile_units(i["sc_w_out_2"][0]))
    return stream


def fill_columns(i):
    at, n = column_places()
    out = np.empty((P, n), np.float32)

    def put(name, v):
        a, w = at[name]
        out[:, a:a + w] = np.asarray(v).reshape(w, P).T

    put("c", i["c"])
    put("c_2", i["c_2"])
    put("c_ctx", i["c_ctx_2"])
    put("final_norm", i["final_norm_w"])
    for l in range(DEPTH):
        put(f"ada_b.{l}", i["ada_b"][l])
        put(f"norm_mix.{l}", i["norm_mix_w"][l])
        put(f"norm_ffn.{l}", i["norm_ffn_w"][l])
        put(f"q_norm.{l}", i["q_norm_w"][l])
        put(f"k_norm.{l}", i["k_norm_w"][l])
        put(f"pool_scale.{l}", i["pool_scale"][l])
        put(f"ada_b_2.{l}", i["ada_b_2"][l])
        for k in range(3):
            put(f"ln_g.{l}.{k}", i["ln_g_2"][l, k])
            put(f"ln_b.{l}.{k}", i["ln_b_2"][l, k])
    for k in range(3):
        put(f"conv.{k}", i["sc_conv_2"][0, k])
    return out


def transposed_tokens(x):
    return np.ascontiguousarray(x[0].T.reshape(KT, P, T).transpose(1, 0, 2))


def skewed_bias(rpb):
    pad = GRID_W - NA_KW
    padded = np.zeros((HEADS2, RPB_H, RPB_W + 2 * pad), np.float32)
    padded[:, :, pad:pad + RPB_W] = rpb
    rows = [padded[:, :, GRID_W - 1 - qc:2 * GRID_W - 1 - qc] for qc in range(GRID_W)]
    return np.stack(rows).reshape(GRID_W, HEADS2, RPB_H * GRID_W)


def kernel(**inputs):
    from contextlib import ExitStack

    import concourse.bacc as bacc
    from concourse.bass_utils import run_bass_kernel_spmd

    i = {k: np.asarray(v) for k, v in inputs.items()}
    arrays = {
        "stream": fill_stream(i), "columns": fill_columns(i), "tables": shape_tables(),
        "x_t": transposed_tokens(i["x"]), "ctx_t": transposed_tokens(i["ctx_2"]), "rpb": skewed_bias(i["na_rpb_2"][0]),
    }
    nc = bacc.Bacc("TRN2", target_bir_lowering=False, num_devices=1)
    args = [nc.dram_tensor(name, a.shape, F32, kind="ExternalInput").ap() for name, a in arrays.items()]
    out = nc.dram_tensor("out_t", (P, KT, T), F32, kind="ExternalOutput").ap()
    with ExitStack() as ctx:
        build(nc, ctx, *args, out)
    r = run_bass_kernel_spmd(nc, [arrays], core_ids=[0])
    y = r.results[0]["out_t"]
    return np.ascontiguousarray(y.transpose(1, 0, 2).reshape(D, T).T)[None]
```

```python
from collections import namedtuple

import numpy as np

import concourse.bass as bass
from concourse import mybir
from concourse.alu_op_type import AluOpType as ALU

F32 = mybir.dt.float32
F32R = mybir.dt.float32r
U32 = mybir.dt.uint32
ACT = mybir.ActivationFunctionType
AX = mybir.AxisListType

P = 128
D = 1024
KT = D // P
T = 256
TT = T // P
DEPTH = 2
GRID_W = 64
EPS = 1e-6
HEADS, KV_HEADS, HEAD_DIM = 8, 2, 128
POOL_GROUPS = 4
POOL_WINDOWS = (2, 4, 8, 16)
W_IN_TILES = 32
PEER_HEADS, TOPK, KEYS = 8, 16, 128
LISTS = 2 * PEER_HEADS
QK_HEADS = HEADS + KV_HEADS
HEADS2, HEAD_DIM2 = 16, 64
FF_TILES = 22
ROWS = T // GRID_W
NA_KW = 16
RPB_H, RPB_W = 15, 31
ALPHA = (2.0 * DEPTH) ** 0.25
MASKED = -1e30

ADA2_GATES = 6
ADA2_CHOICE = (0, 6)
ADA2_FIRST = (0, ADA2_CHOICE[0] + ADA2_GATES)

UNIT = 1024
HALF = UNIT // 2

Stage = namedtuple("Stage", "name units split source q s r g")


def plan():
    rows = []
    sources = {}
    placed = 0

    def add(name, units, split, groups=0, source=None, skip=0):
        nonlocal placed
        if source == "qkv_matrix" and source not in sources:
            sources[source] = placed
            placed += 24
        if source is None:
            sources[name] = placed
            placed += units
            rows.append((name, units, split, sources[name], groups))
        else:
            rows.append((name, units, split, sources[source] + skip, groups))

    add("ada1.0", 48, False)
    for l in range(DEPTH):
        add(f"w_in.{l}", W_IN_TILES, True, W_IN_TILES)
        add(f"pool_mix.{l}", 1, False)
        add(f"attn_o.{l}", KT, True, KT)
        add(f"pool_o.{l}", POOL_GROUPS, True)
        add(f"w_out.{l}", KT, True, KT)
        add(f"query.{l}", 32, True, 32)
        add(f"sub_keys.{l}", 4, False)
        if l == 0:
            add("ada1.1", 48, False)
        if ADA2_CHOICE[l]:
            add(f"ada2_choice.{l}", KT * ADA2_CHOICE[l], False)
        add(f"ada2_gates.{l}", KT * ADA2_GATES, False)
        add(f"experts.{l}", 2 * KEYS, True, KEYS)
    add("ffn.0.0", 3 * FF_TILES, True, FF_TILES)
    add("ffn.0.0.x", 3 * FF_TILES, True, FF_TILES, source="ffn.0.0")
    add("kv_ctx", 16, True, 16, source="qkv_matrix", skip=8)
    add("qkv", 24, True, 24, source="qkv_matrix")
    add("na_o", KT, True, KT)
    add("ffn.0.1", 3 * FF_TILES, True, FF_TILES)
    add("ffn.1.0", 3 * FF_TILES, True, FF_TILES)
    add("conv_in", 24, True, 24)
    add("conv_o", KT, True, KT)
    add("ffn.1.1", 3 * FF_TILES, True, FF_TILES)

    out, q, s, r, g = {}, 0, 0, 0, 0
    for name, units, split, source, groups in rows:
        out[name] = Stage(name, units, split, source, q, s, r, g)
        q += units
        s += units * split
        r += units * (not split)
        g += groups
    return out, placed


COLUMNS = [("c", KT), ("c_2", KT), ("c_ctx", KT), ("final_norm", KT)]
for _l in range(DEPTH):
    COLUMNS += [(f"ada_b.{_l}", 48), (f"norm_mix.{_l}", KT), (f"norm_ffn.{_l}", KT), (f"q_norm.{_l}", 1),
                (f"k_norm.{_l}", 1), (f"pool_scale.{_l}", POOL_GROUPS), (f"ada_b_2.{_l}", 72)]
    for _k in range(3):
        COLUMNS += [(f"ln_g.{_l}.{_k}", KT), (f"ln_b.{_l}.{_k}", KT)]
COLUMNS += [("conv.0", KT), ("conv.1", KT), ("conv.2", KT)]


def operands_made():
    order = []
    for l in range(DEPTH):
        order += [(f"w_in.{l}", KT), (f"attn_o.{l}", KT), (f"pool_o.{l}", POOL_GROUPS), (f"w_out.{l}", KT),
                  (f"query.{l}", KT)]
    order += [(name, KT) for name in ("ffn.0.0", "ffn.0.0.x", "kv_ctx", "qkv", "na_o", "ffn.0.1", "ffn.1.0", "conv_in",
                                      "conv_o", "ffn.1.1")]
    out, n = {}, 0
    for name, tiles_ in order:
        n += tiles_
        out[name] = n
    return out


def column_places():
    at, out = 0, {}
    for name, n in COLUMNS:
        out[name] = (at, n)
        at += n
    return out, at


TABLES = [("ident", P), ("iota", P), ("cos1", T), ("sin1", T), ("swap1", P), ("inv_count", POOL_GROUPS * T),
          ("cos2", T), ("sin2", T), ("cos2_q", T), ("sin2_q", T), ("swap2", P), ("mask", GRID_W)]


def table_places():
    at, out = 0, {}
    for name, n in TABLES:
        out[name] = (at, n)
        at += n
    return out, at


class Steps:

    def __init__(self):
        self.n = 0

    def one(self):
        self.n += 1
        return 1


class Seen:

    def __init__(self):
        self.at = {}

    def __call__(self, name, k=1):
        self.at[name] = self.at.get(name, 0) + k
        return self.at[name]


def build(nc, ctx, stream, columns, tables, x_in, ctx_in, rpb, out):
    stages, _ = plan()
    made = operands_made()
    col_at, n_cols = column_places()
    tab_at, _ = table_places()

    def sb(name, shape, dt=F32):
        return ctx.enter_context(nc.sbuf_tensor(name, shape, dt))

    def sem(name):
        return ctx.enter_context(nc.semaphore(name))

    X = sb("X", [P, KT, T])
    XH = sb("XH", [P, KT, T], F32R)
    XL = sb("XL", [P, KT, T], F32R)
    raw = sb("raw", [P, 4, UNIT])
    wh = sb("wh", [P, 4, HALF], F32R)
    wl = sb("wl", [P, 4, HALF], F32R)
    AH = sb("AH", [P, 2, T], F32R)
    AL = sb("AL", [P, 2, T], F32R)
    AG = sb("AG", [P, 2, T])
    AP_ = sb("AP_", [P, 2, T])
    arena_at = -(-nc.sbuf_base // 32) * 32
    arena = sb("arena", [P, T * KEYS])

    def in_arena(name, shape, at, dt):
        return nc.alloc_sbuf_tensor_at(name, shape, dt, offset=arena_at + 4 * at)
    cols = sb("cols", [P, n_cols])
    ident = sb("ident", [P, P])
    iota = sb("iota", [P, P])
    mean_d = sb("mean_d", [P, P])
    head_pick = sb("head_pick", [P, 2 * QK_HEADS - 1])
    eps = sb("eps", [P, 1])
    cs = sb("cs", [P, 3, KT])
    cs2 = sb("cs2", [P, KT, 2])
    mod1 = sb("mod1", [P, DEPTH, 48])
    mod2 = sb("mod2", [P, DEPTH, 72, 2])
    mod2_flat = mod2[:, :, :, :].rearrange("p l n c -> p (l n c)")
    scale = sb("scale", [P, KT])
    coef = sb("coef", [P, 2, KT])
    view_coef = sb("view_coef", [P, 2, KT])
    routed = sb("routed", [P, 3, T])
    weight_hi = sb("weight_hi", [P, T], F32R)
    MOST_ROWS = 2 * max(ADA2_GATES, *ADA2_CHOICE)
    pick = sb("pick", [P, KT, 2 + MOST_ROWS])
    rows = sb("rows", [MOST_ROWS, UNIT])
    small = sb("small", [P, 64])
    banks = [ctx.enter_context(nc.psum_tensor(f"bank{i}", [P, 512], F32)) for i in range(8)]

    def A(at, n):
        return arena[:, at:at + n]

    def tiles(at, n, w=T):
        return arena[:, at:at + n * w].rearrange("p (n w) -> p n w", w=w)

    def spread(view, n):
        return view.unsqueeze(1).broadcast_to([P, n, view.shape[-1]])

    def column(name, k=0, n=1):
        at = col_at[name][0]
        return cols[:, at + k:at + k + n]

    gates = arena[:, :].rearrange("p (t j) -> p t j", j=KEYS)

    PROJ, SQ, QW, ROT, ROPED, RMS = 0, 8192, 10752, 13312, 15872, 18432
    POOLX = 18944
    VN, PR, PT = 20992, 21504, 22528
    TAB1 = 23552
    PAD, S2, S4, S8, S16, PM = 25216, 26304, 27392, 28208, 28752, 29024
    MODUL, ATTNO = 12288, 8192
    PADW = T + 16
    QUERY, SCORES, REPL, CAND, CREPL, EQ, PICK = 0, 8192, 12288, 14336, 16384, 18432, 20480
    VALS, IDXU, IDXF = 22528, 22784, 23040
    TOPV, TOPU, TOPA, TOPB, TMPU = 23296, 23424, 23552, 23680, 24192
    CHOICES = 24320
    def one_hots(k):
        k = k % 2
        return (wh[:, k, :], (AG, AP_)[k][:, :, :].rearrange("p a w -> p (a w)"), wh[:, 2 + k, :], wl[:, k, :])
    CTX, BIAS, X2H, X2L, TAB2, RMS2 = 0, 2048, 10240, 12288, 14336, 16128
    QT, KTL, VT, KTC, VTC, TMP, VNAT = 16384, 18432, 20480, 22528, 24576, 26624, 28672
    ZSQ = VNAT
    PR2, PT2 = 10240, 12288
    CONV, CU, CT = 16384, 2048, 4352

    first_pair = (XH[:, :, :], XL[:, :, :])
    second_pair = (in_arena("X2H", [P, KT, T], X2H, F32R)[:, :, :], in_arena("X2L", [P, KT, T], X2L, F32R)[:, :, :])
    pool_pair = (in_arena("pool_h", [P, POOL_GROUPS, T], POOLX, F32R)[:, :, :],
                 in_arena("pool_l", [P, POOL_GROUPS, T], POOLX + POOL_GROUPS * T, F32R)[:, :, :])

    cos1, sin1 = A(TAB1, T), A(TAB1 + T, T)
    swap1 = A(TAB1 + 2 * T, P)
    inv_count = tiles(TAB1 + 2 * T + P, POOL_GROUPS)
    cos2, sin2 = A(TAB2, T), A(TAB2 + T, T)
    cos2_q, sin2_q = A(TAB2 + 2 * T, T), A(TAB2 + 3 * T, T)
    swap2 = A(TAB2 + 4 * T, P)
    mask = A(TAB2 + 4 * T + P, GRID_W)
    TURN_BANKS = (0, 1, 2, 3, 6)

    raw_ready = [sem(f"raw_ready{i}") for i in range(4)]
    hi_ready = sem("hi_ready")
    lo_ready = sem("lo_ready")
    halves_free = sem("halves_free")
    raw_used = sem("raw_used")
    group_free = sem("group_free")
    prepared = sem("prepared")
    x_loaded = sem("x_loaded")
    tables_loaded = sem("tables_loaded")
    bias_loaded = sem("bias_loaded")
    stored = sem("stored")
    constants_set = sem("constants_set")
    silu_ready = sem("silu_ready")
    rows_copied = sem("rows_copied")
    picked = sem("picked")
    mod_turned = sem("mod_turned")
    mod_copied = sem("mod_copied")
    mod_ready = sem("mod_ready")
    squares_ready = sem("squares_ready")
    stat_ready = sem("stat_ready")
    rms_ready = sem("rms_ready")
    m_ready = sem("m_ready")
    xh_ready = sem("xh_ready")
    xl_ready = sem("xl_ready")
    centred = sem("centred")
    act_fn = sem("act_fn")
    ah_ready = sem("ah_ready")
    act_ready = sem("act_ready")
    dve_step = sem("dve_step")
    act_step = sem("act_step")
    space_free = sem("space_free")
    x_done = sem("x_done")
    head_squares = sem("head_squares")
    head_sums = sem("head_sums")
    head_rms = sem("head_rms")
    v_transposed = sem("v_transposed")
    v_ready = sem("v_ready")
    weighted = sem("weighted")
    swapped = sem("swapped")
    roped = sem("roped")
    gates_sig = sem("gates_sig")
    scores_ready = sem("scores_ready")
    negmax_ready = sem("negmax_ready")
    exp_done = sem("exp_done")
    probs_ready = sem("probs_ready")
    transposed = sem("transposed")
    pt_copied = sem("pt_copied")
    pv_done = sem("pv_done")
    pool_ready = sem("pool_ready")
    acc_done = sem("acc_done")
    route_scores = sem("route_scores")
    route_evacuated = sem("route_evacuated")
    top_shifted = sem("top_shifted")
    top_exp = sem("top_exp")
    choices_ready = sem("choices_ready")
    choices_turned = sem("choices_turned")
    choices_copied = sem("choices_copied")
    onehots_ready = sem("onehots_ready")
    hot_step = sem("hot_step")
    low_ready = sem("low_ready")
    onehots_free = sem("onehots_free")
    gate_banks_free = sem("gate_banks_free")
    evacuated = sem("evacuated")
    view_step = sem("view_step")
    view_ready = sem("view_ready")
    head_inverse = sem("head_inverse")
    turned_used = sem("turned_used")
    inverse_spread = sem("inverse_spread")
    view_coef_ready = sem("view_coef_ready")

    SLOTS = 4
    BATCH = 4
    BATCHES = T // BATCH
    ROUND = BATCHES // ADA2_GATES // 2 * 2
    REST = range(ROUND * ADA2_GATES, BATCHES)

    block = ctx.enter_context(nc.Block())

    def mod_places(name):
        return 0 if name.startswith("ada1") else 64

    ADA_STAGES = sum(name.startswith("ada") for name in stages)

    def pair_steps(nin):
        count = KEYS if nin == 1 else FF_TILES
        body = 2 if nin == 1 else 4
        rounds = (count - 1) // body
        return count, body, rounds

    @block.sync
    def _(sp):
        seen = Seen()

        def released(unit):
            for st in stages.values():
                if st.q <= unit < st.q + st.units:
                    k = unit - st.q
                    return (lo_ready, 2 * (st.s + k) + 2) if st.split else (raw_used, st.r + k + 1)

        sp.dma_start(cols[:, :], columns).then_inc(prepared, 16)
        sp.dma_start(ident[:, :], tables[:, tab_at["ident"][0]:tab_at["ident"][0] + P]).then_inc(prepared, 16)
        sp.dma_start(iota[:, :], tables[:, tab_at["iota"][0]:tab_at["iota"][0] + P]).then_inc(prepared, 16)
        sp.dma_start(X[:, :, :], x_in).then_inc(x_loaded, 16)

        for st in stages.values():
            for k in range(4 if st.units >= 4 else st.units):
                q = st.q + k
                if q >= 4:
                    sp.wait_ge(*released(q - 4))
                sp.dma_start(raw[:, q % 4, :], stream[st.source + k, :, :]).then_inc(raw_ready[q % 4], 16)
            rounds = (st.units - 4) // 4
            if rounds > 0:
                per = 8 if st.split else 4
                with sp.Fori(0, rounds) as i:
                    for b in range(4):
                        q = st.q + 4 + b
                        s, v = released(q - 4)
                        sp.wait_ge(s, v + per * i)
                        sp.dma_start(raw[:, q % 4:q % 4 + 1, :],
                                     stream[bass.ds(st.source + 4 + b + 4 * i, 1), :, :]
                                     .rearrange("a p n -> p a n")).then_inc(raw_ready[q % 4], 16)
            for k in range(4 + 4 * max(rounds, 0), st.units):
                q = st.q + k
                sp.wait_ge(*released(q - 4))
                sp.dma_start(raw[:, q % 4, :], stream[st.source + k, :, :]).then_inc(raw_ready[q % 4], 16)

        for k in range(0, KT, 2):
            sp.wait_ge(x_done, KT * DEPTH + k + 2)
            sp.dma_start(out[:, k:k + 2, :], X[:, k:k + 2, :]).then_inc(stored, 16)
        sp.wait_ge(stored, 16 * KT // 2)

    @block.gpsimd
    def _(pool):
        pool.memset(mean_d[:, :], 1.0 / D).then_inc(constants_set, 1)
        pool.memset(eps[:, :], EPS).then_inc(constants_set, 1)
        pool.memset(head_pick[:, :], 0.0).then_inc(constants_set, 1)
        pool.wait_ge(constants_set, 3)
        pool.memset(head_pick[:, QK_HEADS - 1:QK_HEADS], 1.0 / HEAD_DIM).then_inc(constants_set, 1)
        at1, _ = tab_at["cos1"]
        at2, _ = tab_at["cos2"]
        picks = [0]
        read_by = [0]

        def pick_vectors(name, nv):
            st = stages[name]
            vectors = cs[:, 0, :].unsqueeze(2) if nv == 1 else cs2[:, :, :]
            zeros = spread(head_pick[:, 0:nv], KT)
            if read_by[0]:
                pool.wait_ge(raw_used, read_by[0])
            pool.memset(pick[:, :, :], 0.0).then_inc(picked, 1)
            pool.wait_ge(picked, picks[0] + 1)
            pool.tensor_copy(pick[:, :, nv:2 * nv], vectors).then_inc(picked, 1)
            with pool.Fori(1, st.units // KT) as i:
                pool.wait_ge(raw_used, st.r + KT * i)
                pool.tensor_copy(pick[:, :, bass.ds(nv * i, nv)], zeros).then_inc(picked, 1)
                pool.tensor_copy(pick[:, :, bass.ds(nv + nv * i, nv)], vectors).then_inc(picked, 1)
            picks[0] += 2 * (st.units // KT)
            read_by[0] = st.r + st.units

        for l in range(DEPTH):
            if l:
                pool.wait_ge(space_free, l)
            pool.dma_start(A(TAB1, 2 * T + P + POOL_GROUPS * T),
                           tables[:, at1:at1 + 2 * T + P + POOL_GROUPS * T]).then_inc(tables_loaded, 16)
            if l == 0:
                pool.wait_ge(silu_ready, 1)
                pick_vectors("ada1.0", 1)
                pick_vectors("ada1.1", 1)
            if ADA2_CHOICE[l]:
                pick_vectors(f"ada2_choice.{l}", 2)
            pick_vectors(f"ada2_gates.{l}", 2)
        pool.wait_ge(space_free, DEPTH)
        pool.dma_start(tiles(CTX, KT), ctx_in).then_inc(tables_loaded, 16)
        pool.dma_start(A(TAB2, 4 * T + P + GRID_W), tables[:, at2:at2 + 4 * T + P + GRID_W]).then_inc(tables_loaded, 16)
        for qb in range(TT):
            for r2 in range(2):
                row = 2 * qb + r2
                dst = arena[64 * r2:64 * r2 + 64, BIAS + qb * HEADS2 * T:BIAS + (qb + 1) * HEADS2 * T]
                pool.dma_start(dst.rearrange("p (h r) -> p h r", h=HEADS2),
                               rpb[:, :, (7 - row) * GRID_W:(7 - row + ROWS) * GRID_W]).then_inc(bias_loaded, 16)
        pool.wait_ge(xl_ready, made["ffn.0.0"])
        pool.tensor_scalar(tiles(CTX, KT), tiles(CTX, KT), ALPHA, None, ALU.mult).then_inc(view_ready, 1)
        for n, name in enumerate(("ffn.0.0.x", "qkv", "ffn.0.1", "ffn.1.0", "conv_in", "ffn.1.1")):
            pool.wait_ge(xl_ready, made[name])
            pool.wait_ge(view_coef_ready, n + 1)
            pool.tensor_tensor(X[:, :, :], X[:, :, :], spread(A(RMS2, T), KT), ALU.mult).then_inc(view_step, 1)
            pool.wait_ge(view_step, n + 1)
            for k in range(KT):
                factor, shift = view_coef[:, 0, k:k + 1], view_coef[:, 1, k:k + 1]
                pool.tensor_scalar(X[:, k, :], X[:, k, :], factor, shift, ALU.mult, ALU.add).then_inc(view_ready, 1)

    @block.scalar
    def _(act):
        seen = Seen()
        steps = Steps()
        raws = {}

        def hi(st, k, i=0, per=0):
            s, q = st.s + k, st.q + k
            for half in range(2):
                if half == 0:
                    act.wait_ge(raw_ready[q % 4], 16 * (q // 4 + 1) + 4 * per * i)
                n = 2 * s + half
                act.wait_ge(halves_free, n + 1 + 2 * per * i)
                act.activation(wh[:, n % 4, :], raw[:, q % 4, HALF * half:HALF * (half + 1)],
                               ACT.Copy).then_inc(hi_ready, 1)

        def group_done(st, k, i=0, per=0):
            act.wait_ge(halves_free, SLOTS + 2 * (st.s + k + 1) + 2 * per * i)

        def product(st, evacuate=None, a=0, b=None, then=None):
            b = st.units if b is None else b
            count = b - a - (b == st.units)

            def take(k, i, per):
                if evacuate is not None:
                    group_done(st, k, i, per)
                    evacuate(k + per * i, banks[4 + (st.g + k) % 2], 2 + st.g + k + 1 + per * i)

            def step(k, i, per):
                hi(st, k + 1, i, per)
                take(k, i, per)

            rounds = count // 4 if count >= 8 else 0
            if rounds:
                with act.Fori(0, rounds) as i:
                    for k in range(a, a + 4):
                        step(k, i, 4)
            for k in range(a + 4 * rounds, a + count):
                step(k, 0, 0)
            if b == st.units:
                if then is not None:
                    hi(then, 0)
                take(b - 1, 0, 0)

        def to_arena(at, func=ACT.Copy, scale=1.0):
            def evacuate(k, bank, released):
                act.activation(arena[:, bass.ds(at + k * T, T)], bank[:, 0:T], func, scale=scale)\
                   .then_inc(group_free, 1)
            return evacuate

        def pairs(st, nin, func, hooks=None, then=None):
            count = KEYS if nin == 1 else FF_TILES
            body = 2 if nin == 1 else 4
            per = nin + 1
            hooks = hooks or {}

            def first(j, i, body):
                for c in range(nin):
                    hi(st, nin + j * per + c, i, body * per)

            def fn(j, i, body):
                group_done(st, nin - 1 if j == 0 else nin + (j - 1) * per + nin - 1, i, body * per)
                act.activation(AG[:, j % 2, :], banks[4 + (st.g + j) % 2][:, 0:T], func).then_inc(act_fn, 1)

            def last(j, i, body):
                hi(st, min(nin + j * per + nin, count * per - 1), i, body * per)

            if nin == 2:
                hi(st, 1)
            if -1 in hooks:
                hooks[-1]()
            peeled = max([0] + list(hooks)) + 1
            for j in range(peeled):
                first(j, 0, 0)
                fn(j, 0, 0)
                last(j, 0, 0)
                if j in hooks:
                    hooks[j]()
            loops = (count - 1 - peeled) // body
            with act.Fori(0, loops) as i:
                for b in range(peeled, peeled + body):
                    first(b, i, body)
                    fn(b, i, body)
                    last(b, i, body)
            for j in range(peeled + loops * body, count - 1):
                first(j, 0, 0)
                fn(j, 0, 0)
                last(j, 0, 0)
            fn(count - 1, 0, 0)
            last(count - 1, 0, 0)
            if then is not None:
                hi(then, 0)

        def operand(ks, source, shift=None, pair=first_pair):
            for k in ks:
                act.wait_ge(m_ready, seen("m_ready"))
                if shift is None:
                    act.activation(pair[0][:, k, :], source[:, k, :], ACT.Copy).then_inc(xh_ready, 1)
                else:
                    act.activation(pair[0][:, k, :], source[:, k, :], ACT.Identity, bias=shift(k)).then_inc(xh_ready, 1)

        def squares(view, sq, semaphore, name):
            for k in range(KT):
                if name is not None:
                    act.wait_ge(semaphore, seen(name))
                act.activation(A(sq + k * T, T), view[:, k, :], ACT.Square).then_inc(squares_ready, 1)

        def root(bank, dst):
            act.wait_ge(stat_ready, seen("stat_ready"))
            act.activation(dst, bank, ACT.Sqrt, bias=eps[:, 0:1]).then_inc(rms_ready, 1)

        act.wait_ge(prepared, 48)
        act.wait_ge(constants_set, 4)
        for k, name in enumerate(("c", "c_2", "c_ctx")):
            last = act.activation(cs[:, k, :], column(name, 0, KT), ACT.Silu)
        last.then_inc(act_step, steps.one())
        act.wait_ge(act_step, steps.n)
        act.activation(cs2[:, :, 0], cs[:, 1, :], ACT.Copy)
        act.activation(cs2[:, :, 1], cs[:, 2, :], ACT.Copy).then_inc(silu_ready, 1)

        def ada(name, nv, dst):
            st = stages[name]
            n = st.units // KT
            act.wait_ge(raw_used, st.r + st.units)
            for half in range(2):
                act.activation(rows[0:nv * n, HALF * half:HALF * (half + 1)],
                               banks[6 + half][0:nv * n, :], ACT.Copy).then_inc(rows_copied, 1)
            act.wait_ge(mod_turned, seen("mod_turned"))
            act.activation(dst.rearrange("p (b f v) -> p f b v", f=KT, v=nv),
                           banks[4][:, 0:nv * n * KT].rearrange("p (f b v) -> p f b v", f=KT, v=nv),
                           ACT.Copy).then_inc(mod_copied, 1)

        def blocks_of(first, n):
            return mod2_flat[:, 2 * KT * first:2 * KT * (first + n)]

        rms = A(RMS, T)
        modul = tiles(MODUL, KT)
        ada("ada1.0", 1, mod1[:, 0, :])
        hi(stages["w_in.0"], 0)
        act.wait_ge(x_loaded, 16)
        for l in range(DEPTH):
            squares(X, SQ, *((x_done, "x_done") if l else (None, None)))
            root(banks[6][:, 0:T], rms)
            operand(range(KT), modul, lambda k: mod1[:, l, k:k + 1])
            st = stages[f"w_in.{l}"]
            product(st, to_arena(PROJ), 0, 12)
            act.wait_ge(group_free, 2 + st.g + QK_HEADS)
            act.activation(tiles(SQ, QK_HEADS), tiles(PROJ, QK_HEADS), ACT.Square).then_inc(head_squares, 1)
            product(st, to_arena(PROJ), 12, 14)
            act.wait_ge(v_transposed, seen("v_transposed"))
            act.activation(A(VN, 512), banks[7][:, :], ACT.Copy).then_inc(v_ready, 1)
            act.wait_ge(head_sums, l + 1)
            act.activation(arena[0:QK_HEADS, RMS:RMS + T], banks[6][0:QK_HEADS, 0:T], ACT.Sqrt,
                           bias=eps[0:QK_HEADS, 0:1]).then_inc(head_rms, 1)
            product(st, to_arena(PROJ), 14, 16)
            product(st, to_arena(PROJ, ACT.Sigmoid), 16, 32, then=stages[f"attn_o.{l}"])

            softmax_scale = float(HEAD_DIM) ** -0.5

            def exps(h):
                hh = l * HEADS + h
                o = (h % 4) * 8
                act.wait_ge(negmax_ready, hh + 1)
                for qb in range(TT):
                    if hh >= 2:
                        act.wait_ge(transposed, hh - 1)
                    act.activation(A(PR + (h % 2) * 512 + qb * T, T), banks[(0, 1, 4, 5)[h % 4]][:, qb * T:(qb + 1) * T],
                                   ACT.Exp, bias=small[:, o + 2 + qb:o + 3 + qb], scale=softmax_scale,
                                   accum_out=small[:, o + 4 + qb:o + 5 + qb]).then_inc(exp_done, 1)

            exps(0)
            exps(1)
            for h in range(HEADS):
                hh = l * HEADS + h
                act.wait_ge(transposed, hh + 1)
                if hh >= 2:
                    act.wait_ge(pv_done, hh - 1)
                act.activation(A(PT + (h % 2) * 512, 512), banks[2 + h % 2][:, :], ACT.Copy).then_inc(pt_copied, 1)
                if h + 2 < HEADS:
                    exps(h + 2)
                act.wait_ge(pv_done, hh + 1)
                act.activation(XH[:, h, :], banks[6 + h % 2][:, 0:T], ACT.Copy).then_inc(xh_ready, 1)
            st = stages[f"attn_o.{l}"]
            product(st, to_arena(ATTNO), 0, 2)
            operand(range(POOL_GROUPS), modul, pair=pool_pair)
            product(st, to_arena(ATTNO), 2, KT, then=stages[f"pool_o.{l}"])
            st = stages[f"pool_o.{l}"]
            for k in range(1, st.units):
                hi(st, k)
            hi(stages[f"w_out.{l}"], 0)
            operand(range(KT), modul)

            def square_tile(k, bank, released):
                act.wait_ge(group_free, released)
                act.activation(arena[:, bass.ds(SQ + k * T, T)].unsqueeze(1), X[:, bass.ds(k, 1), :],
                               ACT.Square).then_inc(squares_ready, 1)
            product(stages[f"w_out.{l}"], square_tile, then=stages[f"query.{l}"])
            root(banks[6][:, 0:T], rms)
            operand(range(KT), modul, lambda k: mod1[:, l, 24 + k:25 + k])
            product(stages[f"query.{l}"], to_arena(QUERY))
            for c in range(4):
                for tt in range(TT):
                    if tt == 0:
                        act.wait_ge(route_scores, seen("route_scores"))
                    else:
                        act.wait_ge(raw_used, stages[f"sub_keys.{l}"].r + c + 1)
                    act.activation(A(SCORES + tt * LISTS * KEYS + c * 512, 512), banks[6 + tt][:, :],
                                   ACT.Copy).then_inc(route_evacuated, 1)
            if l == 0:
                ada("ada1.1", 1, mod1[:, 1, :])
            if ADA2_CHOICE[l]:
                ada(f"ada2_choice.{l}", 2, blocks_of(ADA2_FIRST[l], ADA2_CHOICE[l]))
            for tt in range(TT):
                act.wait_ge(top_shifted, seen("top_shifted"))
                w = A(CHOICES + 384 * tt + 256, P)
                act.activation(w, w, ACT.Exp).then_inc(top_exp, 1)
            first = l * BATCHES

            def lows(k, i=0):
                act.wait_ge(hot_step, first + k + 1 + ROUND * i)
                _, unweighted, _, low = one_hots(k)
                for b in range(BATCH):
                    t = BATCH * (k + ROUND * i) + b
                    last = act.activation(low[:, b * P:(b + 1) * P], unweighted[:, b * P:(b + 1) * P], ACT.Copy,
                                          scale=routed[:, 2, bass.ds(t, 1)])
                last.then_inc(low_ready, 1)

            def spread_gates(k, i=0):
                act.wait_ge(onehots_free, 2 + first + k + 1 + ROUND * i)
                act.activation(arena[:, bass.ds((k + ROUND * i) * BATCH * KEYS, BATCH * KEYS)], banks[k % 2][:, :],
                               ACT.Copy).then_inc(gate_banks_free, 1)
            with act.Fori(0, ADA2_GATES) as i:
                for k in range(ROUND):
                    lows(k, i)
                    if k:
                        spread_gates(k - 1, i)
                spread_gates(ROUND - 1, i)
            for k in REST:
                lows(k)
                spread_gates(k)
            ada(f"ada2_gates.{l}", 2, blocks_of(ADA2_FIRST[l] + ADA2_CHOICE[l], ADA2_GATES))
            hi(stages[f"experts.{l}"], 0)
            pairs(stages[f"experts.{l}"], 1, ACT.Gelu, then=stages["ffn.0.0" if l else "w_in.1"])

        ctx_tiles, modul, rms = tiles(CTX, KT), tiles(TMP, KT), A(RMS2, T)

        def shift_of(l, base, side):
            return lambda k: mod2[:, l, base + k:base + k + 1, side]

        shift = lambda k: coef[:, 1, k:k + 1]

        def stream_root(bank, updates):
            if updates:
                act.wait_ge(view_ready, 1 + KT * updates)
            root(bank, rms)

        def layer_norm(updates):
            seen("stat_ready")
            squares(X, ZSQ, centred, "centred")
            stream_root(banks[7][:, 0:T], updates)

        operand(range(KT), modul, shift_of(0, 0, 1))
        hooks = {0: lambda: squares(X, ZSQ, x_done, "x_done"), 4: lambda: stream_root(banks[6][:, 0:T], 0)}
        for n in range(4):
            hooks[6 + n] = lambda n=n: operand((2 * n, 2 * n + 1), modul, shift_of(0, 0, 0), second_pair)
        pairs(stages["ffn.0.0"], 2, ACT.Silu, hooks, then=stages["ffn.0.0.x"])

        def context_squares():
            seen("stat_ready")
            squares(ctx_tiles, ZSQ, centred, "centred")
        hooks = {1: context_squares, 4: lambda: stream_root(banks[7][:, 0:T], 1)}
        for n in range(4):
            hooks[8 + n] = lambda n=n: operand((2 * n, 2 * n + 1), modul, shift)
        pairs(stages["ffn.0.0.x"], 2, ACT.Silu, hooks, then=stages["kv_ctx"])

        st = stages["kv_ctx"]
        keep = to_arena(KTC)
        product(st, keep, 0, 5)
        seen("stat_ready")
        squares(X, ZSQ, centred, "centred")
        product(st, keep, 5, 9)
        stream_root(banks[7][:, 0:T], 1)
        product(st, keep, 9, 11)
        for n in range(4):
            product(st, keep, 11 + n, 12 + n)
            operand((2 * n, 2 * n + 1), modul, shift, second_pair)
        product(st, keep, 15, 16, then=stages["qkv"])

        def values(kts):
            for kt in kts:
                for c in range(2):
                    act.wait_ge(v_transposed, seen("v_transposed"))
                    act.activation(A(VNAT + kt * D + c * 512, 512), banks[6 + c][:, :], ACT.Copy).then_inc(v_ready, 1)

        st = stages["qkv"]
        product(st, to_arena(QT), 0, 4)
        values((2, 3))
        product(st, to_arena(QT), 4, 24, then=stages["na_o"])
        values((0, 1))

        def exps2(h):
            hh = DEPTH * HEADS + h
            o = (h % 2) * 8
            act.wait_ge(negmax_ready, hh + 1)
            for qb in range(TT):
                if h >= 2:
                    act.wait_ge(transposed, DEPTH * HEADS + 2 * (h - 1))
                act.activation(A(PR2 + (h % 2) * 1024 + qb * 512, 512), banks[4 * (h % 2) + qb][:, :], ACT.Exp,
                               bias=small[:, o + 2 + qb:o + 3 + qb], scale=1.0,
                               accum_out=small[:, o + 4 + qb:o + 5 + qb]).then_inc(exp_done, 1)

        exps2(0)
        exps2(1)
        for h in range(HEADS2):
            hh = DEPTH * HEADS + h
            for half in range(2):
                act.wait_ge(transposed, DEPTH * HEADS + 2 * h + half + 1)
                if h >= 2:
                    act.wait_ge(pv_done, hh - 1)
                act.activation(A(PT2 + (h % 2) * 1024 + half * 512, 512), banks[2 + half][:, :],
                               ACT.Copy).then_inc(pt_copied, 1)
            if h % 2 == 0 and h:
                act.wait_ge(pv_done, hh)
                k = h // 2 - 1
                act.activation(XH[:, k, :], banks[6 + k % 2][:, 0:T], ACT.Copy).then_inc(xh_ready, 1)
            if h + 2 < HEADS2:
                exps2(h + 2)
        act.wait_ge(pv_done, DEPTH * HEADS + HEADS2)
        act.activation(XH[:, KT - 1, :], banks[6 + (KT - 1) % 2][:, 0:T], ACT.Copy).then_inc(xh_ready, 1)
        product(stages["na_o"], then=stages["ffn.0.1"])
        layer_norm(2)
        operand(range(KT), modul, shift)
        pairs(stages["ffn.0.1"], 2, ACT.Silu, then=stages["ffn.1.0"])
        layer_norm(3)
        operand(range(KT), modul, shift)
        pairs(stages["ffn.1.0"], 2, ACT.Silu, then=stages["conv_in"])
        layer_norm(4)
        operand(range(KT), modul, shift)
        product(stages["conv_in"], to_arena(CONV), then=stages["conv_o"])
        operand(range(KT), modul)
        product(stages["conv_o"], then=stages["ffn.1.1"])
        layer_norm(5)
        operand(range(KT), modul, shift)
        pairs(stages["ffn.1.1"], 2, ACT.Silu)
        layer_norm(6)
        for k in range(KT):
            act.wait_ge(centred, seen("centred"))
            act.activation(X[:, k, :], X[:, k, :], ACT.Identity, bias=column("ln_b.1.2", k),
                           scale=column("ln_g.1.2", k)).then_inc(x_done, 1)

    @block.vector
    def _(dve):
        seen = Seen()
        steps = Steps()
        tt_op = dve.tensor_tensor
        MUL, ADD, SUB = ALU.mult, ALU.add, ALU.subtract

        def step(ins):
            ins.then_inc(dve_step, steps.one())

        def settle():
            dve.wait_ge(dve_step, steps.n)

        def lo(st, k, i=0, per=0):
            s, q = st.s + k, st.q + k
            for half in range(2):
                n = 2 * s + half
                dve.wait_ge(hi_ready, n + 1 + 2 * per * i)
                tt_op(wl[:, n % 4, :], raw[:, q % 4, HALF * half:HALF * (half + 1)], wh[:, n % 4, :].bitcast(F32),
                      SUB).then_inc(lo_ready, 1)

        def group_done(st, k, i=0, per=0):
            dve.wait_ge(halves_free, SLOTS + 2 * (st.s + k + 1) + 2 * per * i)

        def product(st, evacuate=None, a=0, b=None, then=None):
            b = st.units if b is None else b
            count = b - a - (b == st.units)

            def take(k, i, per):
                if evacuate is not None:
                    group_done(st, k, i, per)
                    evacuate(k + per * i, banks[4 + (st.g + k) % 2])

            def one(k, i, per):
                lo(st, k + 1, i, per)
                take(k, i, per)

            rounds = count // 4 if count >= 8 else 0
            if rounds:
                with dve.Fori(0, rounds) as i:
                    for k in range(a, a + 4):
                        one(k, i, 4)
            for k in range(a + 4 * rounds, a + count):
                one(k, 0, 0)
            if b == st.units:
                if then is not None:
                    lo(then, 0)
                take(b - 1, 0, 0)

        def residual(factors):
            def evacuate(k, bank):
                dve.scalar_tensor_tensor(X[:, bass.ds(k, 1), :], bank[:, 0:T].unsqueeze(1), factors(k),
                                         X[:, bass.ds(k, 1), :], MUL, ADD).then_inc(group_free, 1)
            return evacuate

        def pairs(st, nin, combine, hooks=None, then=None):
            count = KEYS if nin == 1 else FF_TILES
            body = 2 if nin == 1 else 4
            per = nin + 1
            hooks = hooks or {}

            def first(j, i, body):
                for c in range(nin):
                    lo(st, nin + j * per + c, i, body * per)

            def middle(j, i, body):
                g = st.g + j
                n_act = acts[0] + j
                dve.wait_ge(act_fn, n_act + 1 + body * i)
                combine(j, i, body, banks[4 + g % 2]).then_inc(group_free, 1)
                if j >= 2 or body:
                    k = nin + (j - 2) * per + nin
                    dve.wait_ge(halves_free, SLOTS + 2 * (st.s + k + 1) + 2 * body * per * i)
                dve.wait_ge(group_free, 2 + g + 1 + body * i)
                dve.tensor_copy(AH[:, j % 2, :], AP_[:, j % 2, :]).then_inc(ah_ready, 1)
                dve.wait_ge(ah_ready, n_act + 1 + body * i)
                tt_op(AL[:, j % 2, :], AP_[:, j % 2, :], AH[:, j % 2, :].bitcast(F32), SUB).then_inc(act_ready, 1)

            def last(j, i, body):
                lo(st, min(nin + j * per + nin, count * per - 1), i, body * per)

            if nin == 2:
                lo(st, 1)
            if -1 in hooks:
                hooks[-1]()
            peeled = max([1] + list(hooks)) + 1
            for j in range(peeled):
                first(j, 0, 0)
                middle(j, 0, 0)
                last(j, 0, 0)
                if j in hooks:
                    hooks[j]()
            loops = (count - 1 - peeled) // body
            with dve.Fori(0, loops) as i:
                for b in range(peeled, peeled + body):
                    first(b, i, body)
                    middle(b, i, body)
                    last(b, i, body)
            for j in range(peeled + loops * body, count - 1):
                first(j, 0, 0)
                middle(j, 0, 0)
                last(j, 0, 0)
            middle(count - 1, 0, 0)
            last(count - 1, 0, 0)
            acts[0] += count
            if then is not None:
                lo(then, 0)

        acts = [0]

        def rest(ks, source, shift=None, pair=first_pair):
            for k in ks:
                dve.wait_ge(xh_ready, seen("xh_ready"))
                high = pair[0][:, k, :].bitcast(F32)
                if shift is None:
                    tt_op(pair[1][:, k, :], source[:, k, :], high, SUB).then_inc(xl_ready, 1)
                else:
                    dve.scalar_tensor_tensor(pair[1][:, k, :], source[:, k, :], shift(k), high, ADD,
                                             SUB).then_inc(xl_ready, 1)

        def scaled(ks, src, dst, factor, over=None):
            for k in ks:
                if over is None:
                    ins = dve.tensor_scalar(dst[:, k, :], src[:, k, :], factor(k), None, MUL)
                else:
                    ins = dve.scalar_tensor_tensor(dst[:, k, :], src[:, k, :], factor(k), over, MUL, MUL)
                ins.then_inc(m_ready, 1)

        def operand(src, dst, factor, shift, over=None, pair=first_pair):
            scaled((0, 1), src, dst, factor, over)
            for k in range(KT):
                rest((k,), dst, shift, pair)
                if k + 2 < KT:
                    scaled((k + 2,), src, dst, factor, over)

        def invert(rms):
            dve.wait_ge(rms_ready, seen("rms_ready"))
            step(dve.reciprocal(rms, rms))
            settle()

        def scale_plus_one(dst, src, weight=None):
            step(dve.tensor_scalar(dst, src, 1.0, None, ADD))
            settle()
            if weight is not None:
                step(tt_op(dst, dst, weight, MUL))
                settle()

        def add_bias(l, which, copied):
            dve.wait_ge(mod_copied, copied)
            if which == 1:
                step(tt_op(mod1[:, l, :], mod1[:, l, :], column(f"ada_b.{l}", 0, 48), ADD))
            else:
                b = column(f"ada_b_2.{l}", 0, 72)
                step(tt_op(mod2[:, l, :, :], mod2[:, l, :, :], b.unsqueeze(2).broadcast_to([P, 72, 2]), ADD))
            settle()

        def stream_sum(factor, view, semaphore):
            dve.wait_ge(acc_done, seen("acc_done"))
            for k in range(KT):
                dve.scalar_tensor_tensor(view[:, k, :], banks[k // 2][:, (k % 2) * T:(k % 2 + 1) * T], factor(k),
                                         view[:, k, :], MUL, ADD).then_inc(semaphore, 1)

        def rest_of_head(k):
            dve.wait_ge(xh_ready, seen("xh_ready"))
            tt_op(XL[:, k, :], banks[6 + k % 2][:, 0:T], XH[:, k, :].bitcast(F32), SUB).then_inc(xl_ready, 1)

        dve.wait_ge(prepared, 48)
        X_ = X[:, :, :]
        for l in range(DEPTH):
            if l == 0:
                add_bias(0, 1, 1)
            shift1, scale1, gate1 = (lambda k, a=a: mod1[:, l, a + k:a + k + 1] for a in (0, 8, 16))
            shift2, _, _ = (lambda k, a=a: mod1[:, l, a + k:a + k + 1] for a in (24, 32, 40))
            modul = tiles(MODUL, KT)
            factor = lambda k: scale[:, k:k + 1]
            scale_plus_one(scale[:, :], mod1[:, l, 8:16], column(f"norm_mix.{l}", 0, KT))
            if l == 0:
                lo(stages["w_in.0"], 0)
            invert(A(RMS, T))
            operand(X_, modul, factor, shift1, A(RMS, T))
            st = stages[f"w_in.{l}"]
            product(st, None, 0, 12)
            dve.wait_ge(group_free, 2 + st.g + QK_HEADS)
            dve.wait_ge(tables_loaded, 16 * (l + 1))
            dve.tensor_scalar(A(QW, 8 * T), A(PROJ, 8 * T), column(f"q_norm.{l}"), None, MUL).then_inc(weighted, 1)
            dve.tensor_scalar(A(QW + 8 * T, 2 * T), A(PROJ + 8 * T, 2 * T), column(f"k_norm.{l}"), None,
                              MUL).then_inc(weighted, 1)
            product(st, None, 12, 14)
            dve.wait_ge(weighted, 2 * (l + 1))
            for c in range(2):
                step(tt_op(tiles(ROT + 5 * T * c, 5), tiles(QW + 5 * T * c, 5), spread(cos1, 5), MUL))
                product(st, None, 14 + c, 15 + c)
            dve.wait_ge(head_rms, seen("head_rms"))
            inverse = arena[0:QK_HEADS, RMS:RMS + T]
            dve.reciprocal(inverse, inverse).then_inc(head_inverse, 1)
            product(st, None, 16, 17)
            for c in range(5):
                dve.wait_ge(swapped, seen("swapped"))
                tt_op(tiles(SQ + 512 * c, 2), banks[TURN_BANKS[c]][:, :].rearrange("p (n w) -> p n w", w=T),
                      spread(sin1, 2), MUL).then_inc(turned_used, 1)
                dve.wait_ge(turned_used, 5 * l + c + 1)
                settle()
                step(tt_op(A(ROT + 512 * c, 512), A(ROT + 512 * c, 512), A(SQ + 512 * c, 512), ADD))
                product(st, None, 17 + c, 18 + c)
            settle()
            pad, s2, s4 = tiles(PAD, 4, PADW), tiles(S2, 4, PADW), tiles(S4, 3, PADW)
            s8, s16, pm = tiles(S8, 2, PADW), tiles(S16, 1, PADW), tiles(PM, 4)
            u = tiles(PROJ + 12 * T, 4)
            sums = [
                lambda: dve.memset(A(PAD, 4 * PADW), 0.0),
                lambda: dve.tensor_copy(pad[:, :, 8:8 + T], u),
                lambda: tt_op(s2[:, :, 1:PADW], pad[:, :, 0:PADW - 1], pad[:, :, 1:PADW], ADD),
                lambda: tt_op(s4[:, :, 2:PADW - 1], s2[:, 1:4, 1:PADW - 2], s2[:, 1:4, 3:PADW], ADD),
                lambda: tt_op(s8[:, :, 4:PADW - 3], s4[:, 1:3, 2:PADW - 5], s4[:, 1:3, 6:PADW - 1], ADD)]
            for c in range(5):
                dve.wait_ge(inverse_spread, 5 * l + c + 1)
                tt_op(A(ROPED + 512 * c, 512), A(ROT + 512 * c, 512), banks[TURN_BANKS[c]][:, :],
                      MUL).then_inc(roped, 1)
                step(sums[c]())
                product(st, None, 22 + c, 23 + c)
                settle()
            step(tt_op(s16[:, :, 8:8 + T], s8[:, 1:2, 4:4 + T], s8[:, 1:2, 12:12 + T], ADD))
            product(st, None, 27, 28)
            settle()
            for g, window in enumerate((s2, s4, s8, s16)):
                step(tt_op(pm[:, g, :], window[:, 0, 8:8 + T], inv_count[:, g, :], MUL))
                if g % 2:
                    product(st, None, 28 + g // 2, 29 + g // 2)
            settle()
            tt_op(pm, pm, u, SUB).then_inc(pool_ready, 1)
            product(st, None, 30, 32, then=stages[f"attn_o.{l}"])

            softmax_scale = float(HEAD_DIM) ** -0.5

            def maxes(h):
                hh = l * HEADS + h
                o = (h % 4) * 8
                dve.wait_ge(scores_ready, hh + 1)
                step(dve.reduce_max(small[:, o:o + 2], banks[(0, 1, 4, 5)[h % 4]][:, :].rearrange("p (q k) -> p q k", q=TT), AX.X))
                settle()
                dve.tensor_scalar(small[:, o + 2:o + 4], small[:, o:o + 2], -softmax_scale, None, MUL)\
                   .then_inc(negmax_ready, 1)

            def normalise(h):
                hh = l * HEADS + h
                o = (h % 4) * 8
                dve.wait_ge(exp_done, 2 * (hh + 1))
                step(dve.reciprocal(small[:, o + 6:o + 8], small[:, o + 4:o + 6]))
                settle()
                for qb in range(TT):
                    p = A(PR + (h % 2) * 512 + qb * T, T)
                    dve.tensor_scalar(p, p, small[:, o + 6 + qb:o + 7 + qb], None, MUL).then_inc(probs_ready, 1)

            maxes(0)
            maxes(1)
            normalise(0)
            maxes(2)
            for h in range(HEADS):
                if h + 1 < HEADS:
                    normalise(h + 1)
                if h + 3 < HEADS:
                    maxes(h + 3)
                dve.wait_ge(xh_ready, seen("xh_ready"))
                tt_op(XL[:, h, :], banks[6 + h % 2][:, 0:T], XH[:, h, :].bitcast(F32), SUB).then_inc(xl_ready, 1)
            st = stages[f"attn_o.{l}"]
            product(st, None, 0, 1)
            dve.wait_ge(raw_used, stages[f"pool_mix.{l}"].r + 1)
            for g in range(POOL_GROUPS):
                dve.tensor_scalar(modul[:, g, :], banks[g // 2][:, (g % 2) * T:(g % 2 + 1) * T],
                                  column(f"pool_scale.{l}", g), None, MUL).then_inc(m_ready, 1)
            product(st, None, 1, 3)
            rest(range(POOL_GROUPS), modul, pair=pool_pair)
            product(st, None, 3, KT, then=stages[f"pool_o.{l}"])
            po = stages[f"pool_o.{l}"]
            for k in range(1, po.units):
                lo(po, k)
            lo(stages[f"w_out.{l}"], 0)
            dve.wait_ge(group_free, 2 + st.g + KT)
            step(tt_op(A(ATTNO, KT * T), A(ATTNO, KT * T), A(PROJ + 16 * T, KT * T), MUL))
            dve.wait_ge(acc_done, seen("acc_done"))
            gated_pool = lambda b: step(tt_op(A(PROJ + 24 * T + 512 * b, 512), A(PROJ + 24 * T + 512 * b, 512),
                                              banks[b][:, :], MUL))
            gated_pool(0)
            for b in range(4):
                if b < 3:
                    gated_pool(b + 1)
                dve.wait_ge(dve_step, steps.n - (b < 3))
                for k in (2 * b, 2 * b + 1):
                    tt_op(modul[:, k, :], tiles(ATTNO, KT)[:, k, :], A(PROJ + (24 + k) * T, T), ADD)\
                        .then_inc(m_ready, 1)
                if b:
                    rest((2 * b - 2, 2 * b - 1), modul)
            rest((KT - 2, KT - 1), modul)
            product(stages[f"w_out.{l}"], residual(lambda k: mod1[:, l, bass.ds(16 + k, 1)]),
                    then=stages[f"query.{l}"])
            scale_plus_one(scale[:, :], mod1[:, l, 32:40], column(f"norm_ffn.{l}", 0, KT))
            invert(A(RMS, T))
            operand(X_, modul, factor, shift2, A(RMS, T))
            product(stages[f"query.{l}"], None)

            for tt in range(TT):
                RI, RJ, RW = (CHOICES + 384 * tt + P * n for n in range(3))
                scores = tiles(SCORES + tt * LISTS * KEYS, LISTS, KEYS)
                repl = tiles(REPL, LISTS, KEYS)
                vals, idxf = tiles(VALS, LISTS, TOPK), tiles(IDXF, LISTS, TOPK)
                idxu = A(IDXU, LISTS * TOPK).bitcast(U32).rearrange("p (n w) -> p n w", w=TOPK)
                if tt == 0:
                    dve.wait_ge(route_evacuated, 8 * (l + 1))
                for n in range(LISTS):
                    step(nc.vector.max(vals[:, n, 0:8], scores[:, n, :]))
                settle()
                for n in range(LISTS):
                    step(nc.vector.match_replace(repl[:, n, :], vals[:, n, 0:8], scores[:, n, :], -3e38))
                    step(nc.vector.max_index(idxu[:, n, 0:8], vals[:, n, 0:8], scores[:, n, :]))
                settle()
                for n in range(LISTS):
                    step(nc.vector.max(vals[:, n, 8:16], repl[:, n, :]))
                settle()
                for n in range(LISTS):
                    step(nc.vector.max_index(idxu[:, n, 8:16], vals[:, n, 8:16], repl[:, n, :]))
                settle()
                step(dve.tensor_copy(idxf, idxu))
                cand, crepl = tiles(CAND, PEER_HEADS, 256), tiles(CREPL, PEER_HEADS, 256)
                v4 = A(VALS, LISTS * TOPK).rearrange("p (h two k) -> p h two k", two=2, k=TOPK)
                step(tt_op(A(CAND, 2048).rearrange("p (h a b) -> p h a b", a=TOPK, b=TOPK),
                           v4[:, :, 0, :].unsqueeze(3).broadcast_to([P, PEER_HEADS, TOPK, TOPK]),
                           v4[:, :, 1, :].unsqueeze(2).broadcast_to([P, PEER_HEADS, TOPK, TOPK]), ADD))
                settle()
                topv = tiles(TOPV, PEER_HEADS, TOPK)
                topu = A(TOPU, P).bitcast(U32).rearrange("p (n w) -> p n w", w=TOPK)
                for h in range(PEER_HEADS):
                    step(nc.vector.max(topv[:, h, 0:8], cand[:, h, :]))
                settle()
                for h in range(PEER_HEADS):
                    step(nc.vector.match_replace(crepl[:, h, :], topv[:, h, 0:8], cand[:, h, :], -3e38))
                    step(nc.vector.max_index(topu[:, h, 0:8], topv[:, h, 0:8], cand[:, h, :]))
                settle()
                for h in range(PEER_HEADS):
                    step(nc.vector.max(topv[:, h, 8:16], crepl[:, h, :]))
                settle()
                for h in range(PEER_HEADS):
                    step(nc.vector.max_index(topu[:, h, 8:16], topv[:, h, 8:16], crepl[:, h, :]))
                tt_op(tiles(RW, PEER_HEADS, TOPK), topv, topv[:, :, 0:1].broadcast_to([P, PEER_HEADS, TOPK]),
                      SUB).then_inc(top_shifted, 1)
                settle()
                tmpu = A(TMPU, P).bitcast(U32)
                step(dve.tensor_scalar(tmpu, A(TOPU, P).bitcast(U32), 4, None, ALU.logical_shift_right))
                settle()
                step(dve.tensor_copy(A(TOPA, P), tmpu))
                settle()
                step(dve.tensor_scalar(tmpu, A(TOPU, P).bitcast(U32), 15, None, ALU.bitwise_and))
                settle()
                step(dve.tensor_copy(A(TOPB, P), tmpu))
                settle()
                i4 = A(IDXF, LISTS * TOPK).rearrange("p (h two k) -> p h two k", two=2, k=TOPK)
                eq4 = A(EQ, 2048).rearrange("p (h k a) -> p h k a", k=TOPK, a=TOPK)
                for side, top, dst in ((0, TOPA, RI), (1, TOPB, RJ)):
                    step(tt_op(tiles(EQ, P, TOPK), A(top, P).unsqueeze(2).broadcast_to([P, P, TOPK]),
                               iota[:, 0:TOPK].unsqueeze(1).broadcast_to([P, P, TOPK]), ALU.is_equal))
                    settle()
                    step(tt_op(A(PICK, 2048).rearrange("p (h k a) -> p h k a", k=TOPK, a=TOPK), eq4,
                               i4[:, :, side, :].unsqueeze(2).broadcast_to([P, PEER_HEADS, TOPK, TOPK]), MUL))
                    settle()
                    step(dve.reduce_sum(A(dst, P), tiles(PICK, P, TOPK), AX.X))
            for tt in range(TT):
                dve.wait_ge(top_exp, seen("top_exp"))
                w3 = tiles(CHOICES + 384 * tt + 256, PEER_HEADS, TOPK)
                step(dve.reduce_sum(small[:, 0:PEER_HEADS], w3, AX.X))
                settle()
                step(dve.reciprocal(small[:, 8:8 + PEER_HEADS], small[:, 0:PEER_HEADS]))
                settle()
                tt_op(w3, w3, small[:, 8:16].unsqueeze(2).broadcast_to([P, PEER_HEADS, TOPK]),
                      MUL).then_inc(choices_ready, 1)
                dve.wait_ge(choices_ready, TT * l + tt + 1)
            for tt in range(TT):
                tokens = slice(tt * P, (tt + 1) * P)
                dve.wait_ge(choices_turned, seen("choices_turned"))
                bank = banks[(5, 2)[tt]]
                step(dve.tensor_copy(routed[:, 0:2, tokens], bank[:, 0:2 * P].rearrange("p (n w) -> p n w", w=P)))
                step(dve.tensor_copy(weight_hi[:, tokens], bank[:, 2 * P:3 * P]))
                settle()
                step(tt_op(routed[:, 2, tokens], bank[:, 2 * P:3 * P], weight_hi[:, tokens].bitcast(F32), SUB))
            settle()

            def over_tokens(view, t):
                return view[:, bass.ds(t, BATCH)].unsqueeze(2).broadcast_to([P, BATCH, P])

            def batch(view):
                return view.rearrange("p (t w) -> p t w", w=P)

            first = l * BATCHES
            with dve.Fori(0, BATCHES // 2) as i:
                for k in range(2):
                    t = BATCH * k + 2 * BATCH * i
                    hot_j, unweighted, high, _ = one_hots(k)
                    dve.wait_ge(onehots_free, first + k + 1 + 2 * i)
                    keys = spread(iota[:, :], BATCH)
                    tt_op(batch(unweighted), keys, over_tokens(routed[:, 0, :], t), ALU.is_equal)\
                        .then_inc(hot_step, 1)
                    tt_op(batch(hot_j), keys, over_tokens(routed[:, 1, :], t), ALU.is_equal)
                    dve.wait_ge(hot_step, first + k + 1 + 2 * i)
                    tt_op(batch(high), batch(unweighted), over_tokens(weight_hi[:, :].bitcast(F32), t),
                          MUL).then_inc(onehots_ready, 1)

            def gate(j, i, body, bank):
                return tt_op(AP_[:, j % 2, :].unsqueeze(2), AG[:, j % 2, :].unsqueeze(2),
                             gates[:, :, bass.ds(j + body * i, 1)], MUL)
            st = stages[f"experts.{l}"]
            first_gate = 2 + BATCHES * (l + 1)
            dve.wait_ge(gate_banks_free, first_gate)
            lo(st, 0)
            pairs(st, 1, gate, then=stages["ffn.0.0" if l else "w_in.1"])
            dve.sem_inc(space_free, 1)
            if l == 0:
                add_bias(1, 1, 2)
                stream_sum(lambda k: mod1[:, 0, 40 + k:41 + k], X_, x_done)

        ctx_tiles, modul, rms = tiles(CTX, KT), tiles(TMP, KT), A(RMS2, T)
        factor, shift = (lambda k: coef[:, 0, k:k + 1]), (lambda k: coef[:, 1, k:k + 1])

        def modulation(l, base, n, side):
            return mod2[:, l, base + 8 * n:base + 8 * (n + 1), side]

        def operand_coefficients(l, base, side, weight, bias=None):
            step(dve.tensor_scalar(coef[:, 0, :], modulation(l, base, 1, side), 1.0, None, ADD))
            settle()
            if bias is not None:
                step(tt_op(coef[:, 1, :], column(bias, 0, KT), coef[:, 0, :], MUL))
                settle()
                step(tt_op(coef[:, 1, :], coef[:, 1, :], modulation(l, base, 0, side), ADD))
            else:
                step(dve.tensor_copy(coef[:, 1, :], modulation(l, base, 0, side)))
            if weight is not None:
                step(tt_op(coef[:, 0, :], coef[:, 0, :], column(weight, 0, KT), MUL))
            settle()

        def stream_coefficients(weight, bias=None):
            step(dve.tensor_scalar(view_coef[:, 0, :], column(weight, 0, KT), ALPHA, None, MUL))
            if bias is None:
                dve.memset(view_coef[:, 1, :], 0.0).then_inc(view_coef_ready, 1)
            else:
                dve.tensor_scalar(view_coef[:, 1, :], column(bias, 0, KT), ALPHA, None, MUL)\
                    .then_inc(view_coef_ready, 1)
            settle()

        def residual_factor(l, base, side, res):
            step(dve.tensor_scalar(scale[:, :], modulation(l, base, 2, side), res, None, MUL))
            settle()

        def centre(view, tile_wise=True):
            dve.wait_ge(stat_ready, seen("stat_ready"))
            for k in range(KT):
                tt_op(view[:, k, :], view[:, k, :], banks[6][:, 0:T], SUB).then_inc(centred, 1)
            seen("stat_ready")

        def ffn_combine(j, i, body, bank):
            return tt_op(AP_[:, j % 2, :], AG[:, j % 2, :], bank[:, T:2 * T], MUL)

        for l in range(DEPTH):
            add_bias(l, 2, ADA_STAGES)
        operand_coefficients(0, 0, 1, None)
        dve.wait_ge(tables_loaded, 64)
        operand(ctx_tiles, modul, factor, lambda k: mod2[:, 0, k:k + 1, 1])
        seen("stat_ready", 2 * DEPTH + 1)

        def last_experts():
            stream_sum(lambda k: mod1[:, DEPTH - 1, 40 + k:41 + k], X_, x_done)

        def pieces(at, src, over, shift, pair):
            out = {}
            for n in range(5):
                def piece(n=n):
                    if n:
                        rest((2 * n - 2, 2 * n - 1), modul, shift, pair)
                    if n < 4:
                        scaled((2 * n, 2 * n + 1), src, modul, factor, over)
                out[at + n] = piece
            return out

        def first_coefficients():
            operand_coefficients(0, 0, 0, "final_norm")
            stream_coefficients("final_norm")
            invert(rms)
        hooks = {-1: last_experts, 5: first_coefficients}
        hooks.update(pieces(6, X_, rms, lambda k: mod2[:, 0, k:k + 1, 0], second_pair))
        pairs(stages["ffn.0.0"], 2, ffn_combine, hooks, then=stages["ffn.0.0.x"])
        residual_factor(0, 0, 1, 0.5)
        dve.wait_ge(view_ready, 1)

        def context_sum():
            stream_sum(factor_of_sum, ctx_tiles, evacuated)

        factor_of_sum = lambda k: scale[:, k:k + 1]

        def context_inverse():
            invert(rms)
            operand_coefficients(0, 24, 1, "ln_g.0.0", "ln_b.0.0")

        def context_normed():
            step(tt_op(ctx_tiles, ctx_tiles, spread(rms, KT), MUL))
            settle()
        hooks = {-1: context_sum, 0: lambda: centre(ctx_tiles), 5: context_inverse, 6: context_normed}
        hooks.update(pieces(8, ctx_tiles, None, shift, first_pair))
        pairs(stages["ffn.0.0.x"], 2, ffn_combine, hooks, then=stages["kv_ctx"])
        residual_factor(0, 0, 0, 0.5)
        st = stages["kv_ctx"]
        product(st, None, 0, 1)
        dve.wait_ge(view_ready, 1 + KT)
        stream_sum(factor_of_sum, X_, evacuated)
        product(st, None, 1, 3)
        operand_coefficients(0, 24, 0, "ln_g.0.0", "ln_b.0.0")
        stream_coefficients("ln_g.0.0", "ln_b.0.0")
        centre(X_)
        product(st, None, 3, 9)
        invert(rms)
        product(st, None, 9, 11)
        for n, piece in pieces(11, X_, rms, shift, second_pair).items():
            piece()
            product(st, None, n, n + 1, then=stages["qkv"])
        st = stages["qkv"]
        dve.wait_ge(bias_loaded, 16 * TT * 2)
        both = A(BIAS, TT * HEADS2 * T).rearrange("p (n c) -> p n c", c=GRID_W)
        eighth = TT * HEADS2 * ROWS // 8
        for n in range(8):
            part = both[:, n * eighth:(n + 1) * eighth, :]
            step(tt_op(part, part, spread(mask, eighth), ADD))
            product(st, None, n, n + 1)
        product(st, None, 8, 10)

        def rope2(at, cos, sin, c, n):
            x = tiles(at + 512 * c, 2)
            step(tt_op(tiles(TMP, 2), x, spread(cos, 2), MUL))
            settle()
            dve.wait_ge(swapped, seen("swapped"))
            tt_op(x, banks[c][:, :].rearrange("p (n w) -> p n w", w=T), spread(sin, 2), MUL).then_inc(turned_used, 1)
            dve.wait_ge(turned_used, 5 * DEPTH + n + 1)
            tt_op(x, x, tiles(TMP, 2), ADD).then_inc(roped, 1)
            dve.wait_ge(roped, 5 * DEPTH + n + 1)
        for c, (a, b) in enumerate(((10, 12), (12, 13), (13, 15), (15, 18))):
            rope2(QT, cos2_q, sin2_q, c, c)
            product(st, None, a, b)
        for c, (a, b) in enumerate(((18, 20), (20, 21), (21, 23), (23, 24))):
            rope2(KTL, cos2, sin2, c, 4 + c)
            product(st, None, a, b, then=stages["na_o"])

        def maxes2(h):
            o = (h % 2) * 8
            for qb in range(TT):
                bank = banks[4 * (h % 2) + qb]
                dve.wait_ge(scores_ready, DEPTH * HEADS + 2 * h + qb + 1)
                step(tt_op(bank[:, 0:T], bank[:, 0:T], A(BIAS + (qb * HEADS2 + h) * T, T), ADD))
            for qb in range(TT):
                dve.wait_ge(dve_step, steps.n - 1)
                step(dve.reduce_max(small[:, o + qb:o + qb + 1], banks[4 * (h % 2) + qb][:, :], AX.X))
            settle()
            dve.tensor_scalar(small[:, o + 2:o + 4], small[:, o:o + 2], -1.0, None, MUL).then_inc(negmax_ready, 1)

        def normalise2(h):
            o = (h % 2) * 8
            dve.wait_ge(exp_done, 2 * (DEPTH * HEADS + h + 1))
            step(dve.reciprocal(small[:, o + 6:o + 8], small[:, o + 4:o + 6]))
            settle()
            for qb in range(TT):
                p = A(PR2 + (h % 2) * 1024 + qb * 512, 512)
                dve.tensor_scalar(p, p, small[:, o + 6 + qb:o + 7 + qb], None, MUL).then_inc(probs_ready, 1)

        maxes2(0)
        maxes2(1)
        normalise2(0)
        for h in range(HEADS2):
            if h + 1 < HEADS2:
                normalise2(h + 1)
            if h % 2 == 0 and h:
                k = h // 2 - 1
                rest_of_head(k)
            if h + 2 < HEADS2:
                maxes2(h + 2)
        rest_of_head(KT - 1)
        dve.wait_ge(view_ready, 1 + 2 * KT)
        residual_factor(0, 24, 0, 1.0)

        def layer_norm(l, which, next_l, next_base):
            name = (f"ln_g.{l}.{which}", f"ln_b.{l}.{which}")
            operand_coefficients(next_l, next_base, 0, *name)
            stream_coefficients(*name)
            centre(X_)
            invert(rms)
            operand(X_, modul, factor, shift, rms)

        def ffn(name, l, which, updates, then):
            pairs(stages[name], 2, ffn_combine, then=then)
            residual_factor(l, 0 if which == 0 else 48, 0, 0.5)
            dve.wait_ge(view_ready, 1 + KT * updates)
            stream_sum(factor_of_sum, X_, evacuated)

        product(stages["na_o"], residual(lambda k: scale[:, bass.ds(k, 1)]), then=stages["ffn.0.1"])
        layer_norm(0, 1, 0, 48)
        ffn("ffn.0.1", 0, 2, 3, stages["ffn.1.0"])
        layer_norm(0, 2, 1, 0)
        ffn("ffn.1.0", 1, 0, 4, stages["conv_in"])
        layer_norm(1, 0, 1, 24)
        st = stages["conv_in"]
        cu, conv = tiles(CU, KT, T + 2), tiles(CT, KT)
        b_gate, c_gate, hv = tiles(CONV, KT), tiles(CONV + 8 * T, KT), tiles(CONV + 16 * T, KT)
        product(st, None, 0, 12)
        step(dve.memset(A(CU, KT * (T + 2)), 0.0))
        settle()
        product(st, None, 12, 17)

        def convolve(k):
            dve.wait_ge(group_free, 2 + st.g + 16 + k + 1)
            step(tt_op(cu[:, k, 1:1 + T], c_gate[:, k, :], hv[:, k, :], MUL))
            settle()
            step(dve.tensor_scalar(conv[:, k, :], cu[:, k, 0:T], column("conv.0", k), None, MUL))
            for tap in (1, 2):
                settle()
                step(dve.scalar_tensor_tensor(conv[:, k, :], cu[:, k, tap:tap + T], column(f"conv.{tap}", k),
                                              conv[:, k, :], MUL, ADD))
            settle()
            tt_op(modul[:, k, :], conv[:, k, :], b_gate[:, k, :], MUL).then_inc(m_ready, 1)
        for k in range(KT - 1):
            product(st, None, 17 + k, 18 + k, then=stages["conv_o"])
            convolve(k)
        rest((0, 1, 2, 3, 4, 5), modul)
        convolve(KT - 1)
        rest((6, 7), modul)
        dve.wait_ge(view_ready, 1 + 5 * KT)
        residual_factor(1, 24, 0, 1.0)
        product(stages["conv_o"], residual(lambda k: scale[:, bass.ds(k, 1)]), then=stages["ffn.1.1"])
        layer_norm(1, 1, 1, 48)
        ffn("ffn.1.1", 1, 2, 6, None)
        centre(X_)
        invert(rms)
        for k in range(KT):
            tt_op(X[:, k, :], X[:, k, :], rms, MUL).then_inc(centred, 1)

    @block.tensor
    def _(pe):
        seen = Seen()
        acts = [0]
        pe.sem_inc(halves_free, SLOTS)
        pe.sem_inc(onehots_free, 2)
        pe.sem_inc(group_free, 2)
        pe.sem_inc(gate_banks_free, 2)

        def three(out, n, a, b, moving_h, moving_l, start, stop, check=False):
            pe.matmul(out, wh[:, n % 4, a:b], moving_h, start=start, stop=False, skip_group_check=check)
            pe.matmul(out, wh[:, n % 4, a:b], moving_l, start=False, stop=False, skip_group_check=check)
            return pe.matmul(out, wl[:, n % 4, a:b], moving_h, start=False, stop=stop, skip_group_check=check)

        def tile(st, k, i, per, out, pair):
            awaited = st.name in made and k == 0 and per == 0
            for half in range(2):
                n = 2 * (st.s + k) + half
                pe.wait_ge(lo_ready, n + 1 + 2 * per * i)
                for kk in range(4):
                    kt = 4 * half + kk
                    if awaited:
                        pe.wait_ge(xl_ready, made[st.name] - KT + kt + 1)
                    last = three(out, n, P * kk, P * (kk + 1), pair[0][:, kt, :], pair[1][:, kt, :], kt == 0,
                                 kt == KT - 1)
                last.then_inc(halves_free, 1)

        def product(st, a=0, b=None, pair=first_pair):
            b = st.units if b is None else b

            def one(k, i, per):
                pe.wait_ge(group_free, st.g + k + 1 + per * i)
                tile(st, k, i, per, banks[4 + (st.g + k) % 2][:, 0:T], pair)

            if a == 0:
                one(0, 0, 0)
                a = 1
            rounds = (b - a) // 4 if b - a >= 8 else 0
            if rounds:
                with pe.Fori(0, rounds) as i:
                    for k in range(a, a + 4):
                        one(k, i, 4)
            for k in range(a + 4 * rounds, b):
                one(k, 0, 0)

        def outer(st, k, i, per, moving_h, moving_l, first, final):
            for half in range(2):
                n = 2 * (st.s + k) + half
                pe.wait_ge(lo_ready, n + 1 + 2 * per * i)
                for kk in range(4):
                    o = 4 * half + kk
                    last = three(banks[o // 2][:, (o % 2) * T:(o % 2 + 1) * T], n, P * kk, P * (kk + 1), moving_h,
                                 moving_l, first and o % 2 == 0, final and o % 2 == 1, True)
                last.then_inc(halves_free, 1)

        def pairs(st, nin, hooks=None, pair=first_pair, before_acc=None):
            count = KEYS if nin == 1 else FF_TILES
            body = 2 if nin == 1 else 4
            per = nin + 1
            hooks = hooks or {}

            def first(j, i, body):
                g = st.g + j + 1
                pe.wait_ge(group_free, g + 1 + body * i)
                for c in range(nin):
                    tile(st, nin + j * per + c if j >= 0 else c, i, body * per, banks[4 + g % 2][:, c * T:(c + 1) * T],
                         pair)

            def last(j, i, body, start=False, final=False):
                pe.wait_ge(act_ready, acts[0] + j + 1 + body * i)
                outer(st, min(nin + j * per + nin, count * per - 1), i, body * per, AH[:, j % 2, :], AL[:, j % 2, :],
                      start, final)

            first(-1, 0, 0)
            if -1 in hooks:
                hooks[-1]()
            peeled = max([0] + list(hooks)) + 1
            for j in range(peeled):
                first(j, 0, 0)
                if j == 0 and before_acc is not None:
                    before_acc()
                last(j, 0, 0, start=j == 0)
                if j in hooks:
                    hooks[j]()
            loops = (count - 1 - peeled) // body
            with pe.Fori(0, loops) as i:
                for b in range(peeled, peeled + body):
                    first(b, i, body)
                    last(b, i, body)
            for j in range(peeled + loops * body, count - 1):
                first(j, 0, 0)
                last(j, 0, 0)
            last(count - 1, 0, 0, final=True)
            acts[0] += count

        def finish_acc():
            pe.drain().then_inc(acc_done, 1)

        def column_mean(view, bank, semaphore, name):
            for k in range(KT):
                pe.wait_ge(semaphore, seen(name))
                last = pe.matmul(bank[:, 0:T], mean_d[:, :], view[:, k, :], start=k == 0, stop=k == KT - 1)
            last.then_inc(stat_ready, 1)

        def mean_square(sq, bank):
            column_mean(tiles(sq, KT), bank, squares_ready, "squares_ready")

        blocks = [0]
        ada_stages = [0]

        def rows_times(st, nv, kt, halves=(0, 1), i=0, first=False, last=False):
            q = st.q + kt
            n_rows = nv * st.units // KT
            if kt == 0 and halves[0] == 0:
                pe.wait_ge(picked, 2 * (blocks[0] + 1) + 2 * i)
            if halves[0] == 0:
                pe.wait_ge(raw_ready[q % 4], 16 * (q // 4 + 1) + 32 * i)
            for half in halves:
                matmul = pe.matmul(banks[6 + half][0:n_rows, :], pick[:, kt, nv:nv + n_rows],
                                   raw[:, q % 4, HALF * half:HALF * (half + 1)],
                                   start=first and kt == 0, stop=last and kt == KT - 1)
            if halves[-1] == 1:
                matmul.then_inc(raw_used, 1)

        def rows_free():
            if ada_stages[0]:
                pe.wait_ge(rows_copied, 2 * ada_stages[0])

        def turn(st, nv):
            n_rows = nv * st.units // KT
            blocks[0] += st.units // KT
            ada_stages[0] += 1
            pe.wait_ge(rows_copied, 2 * ada_stages[0])
            if ada_stages[0] > 1:
                pe.wait_ge(mod_copied, ada_stages[0] - 1)
            for f in range(KT):
                last = pe.matmul(banks[4][:, f * n_rows:(f + 1) * n_rows], rows[0:n_rows, f * P:(f + 1) * P],
                                 ident[0:n_rows, 0:n_rows], start=True, stop=True)
            last.then_inc(mod_turned, 1)

        def ada(name, nv):
            st = stages[name]
            n = st.units // KT
            rows_free()
            for kt in range(KT):
                rows_times(st, nv, kt, first=True)
            with pe.Fori(1, n - 1) as i:
                for kt in range(KT):
                    rows_times(st, nv, kt, i=i)
            for kt in range(KT):
                rows_times(st, nv, kt, i=n - 1, last=True)
            turn(st, nv)

        pe.wait_ge(silu_ready, 1)
        ada("ada1.0", 1)
        pe.wait_ge(mod_copied, ada_stages[0])
        for l in range(DEPTH):
            mean_square(SQ, banks[6])
            st = stages[f"w_in.{l}"]
            product(st, 0, 14)
            pe.wait_ge(group_free, 2 + st.g + 12)
            for g in range(KV_HEADS):
                for kt in range(TT):
                    last = pe.transpose(banks[7][:, (g * 2 + kt) * P:(g * 2 + kt + 1) * P],
                                        A(PROJ + (10 + g) * T + kt * P, P), ident[:, :])
            last.then_inc(v_transposed, 1)
            pe.wait_ge(head_squares, l + 1)
            for h in range(QK_HEADS):
                last = pe.matmul(banks[6][0:QK_HEADS, 0:T], head_pick[:, QK_HEADS - 1 - h:2 * QK_HEADS - 1 - h],
                                 A(SQ + h * T, T), start=h == 0, stop=h == QK_HEADS - 1)
            last.then_inc(head_sums, 1)
            product(st, 14, 16)
            pe.wait_ge(weighted, 2 * (l + 1))
            for c in range(5):
                if c == 4:
                    product(st, 16, 17)
                    pe.wait_ge(head_rms, l + 1)
                pe.matmul(banks[TURN_BANKS[c]][:, :], swap1, A(QW + 512 * c, 512), start=True,
                          stop=True).then_inc(swapped, 1)
            product(st, 17, 20)
            pe.wait_ge(head_inverse, l + 1)
            for c in range(5):
                pe.wait_ge(turned_used, 5 * l + c + 1)
                for h in (2 * c, 2 * c + 1):
                    last = pe.matmul(banks[TURN_BANKS[c]][:, (h % 2) * T:(h % 2 + 1) * T],
                                     ident[0:QK_HEADS, h:h + 1].broadcast_to([QK_HEADS, P]),
                                     arena[0:QK_HEADS, RMS:RMS + T], start=True, stop=True)
                last.then_inc(inverse_spread, 1)
                product(st, 20 + c, 21 + c)
            product(st, 25, 32)

            def scores(h):
                for qb in range(TT):
                    last = pe.matmul(banks[(0, 1, 4, 5)[h % 4]][:, qb * T:(qb + 1) * T], A(ROPED + h * T + qb * P, P),
                                     A(ROPED + (8 + h // 4) * T, T), start=True, stop=True)
                last.then_inc(scores_ready, 1)

            def turn_probs(h):
                hh = l * HEADS + h
                pe.wait_ge(probs_ready, 2 * (hh + 1))
                if h >= 2:
                    pe.wait_ge(pt_copied, hh - 1)
                for qb in range(TT):
                    for kt in range(TT):
                        last = pe.transpose(banks[2 + h % 2][:, kt * T + qb * P:kt * T + (qb + 1) * P],
                                            A(PR + (h % 2) * 512 + qb * T + kt * P, P), ident[:, :])
                last.then_inc(transposed, 1)

            pe.wait_ge(roped, 5 * (l + 1))
            pe.wait_ge(v_ready, l + 1)
            pe.wait_ge(group_free, 2 + st.g + W_IN_TILES)
            for h in range(3):
                scores(h)
            turn_probs(0)
            for h in range(HEADS):
                hh = l * HEADS + h
                if h + 3 < HEADS:
                    if h:
                        pe.wait_ge(exp_done, 2 * hh)
                    scores(h + 3)
                pe.wait_ge(pt_copied, hh + 1)
                if h >= 2:
                    pe.wait_ge(xl_ready, made[f"attn_o.{l}"] - HEADS + h - 1)
                for kt in range(TT):
                    last = pe.matmul(banks[6 + h % 2][:, 0:T], A(VN + (h // 4) * T + kt * P, P),
                                     A(PT + (h % 2) * 512 + kt * T, T), start=kt == 0, stop=kt == TT - 1)
                last.then_inc(pv_done, 1)
                if h + 1 < HEADS:
                    turn_probs(h + 1)
            pm = stages[f"pool_mix.{l}"]
            pe.wait_ge(raw_ready[pm.q % 4], 16 * (pm.q // 4 + 1))
            pe.wait_ge(pool_ready, l + 1)
            for g in range(POOL_GROUPS):
                last = pe.matmul(banks[g // 2][:, (g % 2) * T:(g % 2 + 1) * T], raw[:, pm.q % 4, g * P:(g + 1) * P],
                                 A(PM + g * T, T), start=True, stop=True)
            last.then_inc(raw_used, 1)
            product(stages[f"attn_o.{l}"])
            st = stages[f"pool_o.{l}"]
            pe.wait_ge(xl_ready, made[f"pool_o.{l}"])
            for k in range(POOL_GROUPS):
                outer(st, k, 0, 0, pool_pair[0][:, k, :], pool_pair[1][:, k, :], k == 0, k == POOL_GROUPS - 1)
            finish_acc()
            product(stages[f"w_out.{l}"])
            mean_square(SQ, banks[6])
            product(stages[f"query.{l}"])
            st = stages[f"sub_keys.{l}"]
            pe.wait_ge(group_free, 2 + stages[f"query.{l}"].g + 32)
            for c in range(4):
                q = st.q + c
                pe.wait_ge(raw_ready[q % 4], 16 * (q // 4 + 1))
                for tt in range(TT):
                    if c:
                        pe.wait_ge(route_evacuated, 8 * l + 2 * (c - 1) + tt + 1)
                    for n in range(4):
                        for dt in range(2):
                            last = pe.matmul(banks[6 + tt][:, n * P:(n + 1) * P],
                                             A(QUERY + (2 * (4 * c + n) + dt) * T + tt * P, P),
                                             raw[:, q % 4, (2 * n + dt) * P:(2 * n + dt + 1) * P],
                                             start=dt == 0, stop=dt == 1)
                    last.then_inc(route_scores if tt == 0 else raw_used, 1)
            pe.wait_ge(route_evacuated, 8 * (l + 1))
            if l == 0:
                ada("ada1.1", 1)
            if ADA2_CHOICE[l]:
                ada(f"ada2_choice.{l}", 2)
            for tt in range(TT):
                pe.wait_ge(choices_ready, seen("choices_ready"))
                for n in range(3):
                    last = pe.transpose(banks[(5, 2)[tt]][:, n * P:(n + 1) * P], A(CHOICES + 384 * tt + n * P, P),
                                        ident[:, :])
                last.then_inc(choices_turned, 1)
            st = stages[f"ada2_gates.{l}"]
            first = l * BATCHES
            rows_free()

            def spread_choices(k, i=0):
                hot_j, _, high, low = one_hots(k)
                pe.wait_ge(gate_banks_free, first + k + 1 + ROUND * i)
                pe.wait_ge(onehots_ready, first + k + 1 + ROUND * i)
                pe.wait_ge(low_ready, first + k + 1 + ROUND * i)
                for b in range(BATCH):
                    at = slice(b * P, (b + 1) * P)
                    pe.matmul(banks[k % 2][:, at], high[:, at], hot_j[:, at], start=True, stop=False)
                    last = pe.matmul(banks[k % 2][:, at], low[:, at], hot_j[:, at], start=False, stop=True)
                last.then_inc(onehots_free, 1)

            def round_of_batches(i, **ends):
                for k in range(ROUND):
                    spread_choices(k, i)
                    for n in range(2 * KT * k // ROUND, 2 * KT * (k + 1) // ROUND):
                        rows_times(st, 2, n // 2, (n % 2,), i, **ends)
            round_of_batches(0, first=True)
            with pe.Fori(1, ADA2_GATES - 1) as i:
                round_of_batches(i)
            round_of_batches(ADA2_GATES - 1, last=True)
            for k in REST:
                spread_choices(k)
            turn(st, 2)
            pe.wait_ge(mod_copied, ada_stages[0])
            pairs(stages[f"experts.{l}"], 1)
            finish_acc()

        ctx_tiles, X_ = tiles(CTX, KT), X[:, :, :]

        def sum_read():
            pe.wait_ge(evacuated, seen.at["evacuated"])

        pairs(stages["ffn.0.0"], 2, {3: lambda: mean_square(ZSQ, banks[6])},
              before_acc=lambda: pe.wait_ge(x_done, KT * DEPTH))
        finish_acc()
        pairs(stages["ffn.0.0.x"], 2,
              {-1: lambda: column_mean(ctx_tiles, banks[6], evacuated, "evacuated"),
               3: lambda: mean_square(ZSQ, banks[7])}, second_pair, sum_read)
        finish_acc()
        st = stages["kv_ctx"]
        product(st, 0, 3)
        column_mean(X_, banks[6], evacuated, "evacuated")
        product(st, 3, 8)
        mean_square(ZSQ, banks[7])
        product(st, 8, 16)

        def values(kts):
            for kt in kts:
                src = VT if kt < 2 else VTC
                for c in range(2):
                    if kt != 2:
                        pe.wait_ge(v_ready, 2 + 2 * ((kt + 2) % 4 - 1) + c + 1)
                    for f in range(4):
                        last = pe.transpose(banks[6 + c][:, f * P:(f + 1) * P],
                                            A(src + (4 * c + f) * T + (kt % 2) * P, P), ident[:, :])
                    last.then_inc(v_transposed, 1)

        def swap(at, c, n):
            if n >= 4:
                pe.wait_ge(turned_used, 5 * DEPTH + n - 3)
            pe.matmul(banks[c][:, :], swap2, A(at + 512 * c, 512), start=True, stop=True).then_inc(swapped, 1)

        product(stages["qkv"], 0, 4, second_pair)
        pe.wait_ge(rms_ready, 2 * DEPTH + 3)
        pe.wait_ge(centred, 2 * KT)
        pe.wait_ge(group_free, 2 + st.g + 16)
        values((2, 3))
        st = stages["qkv"]
        product(st, 4, 10, second_pair)
        pe.wait_ge(group_free, 2 + st.g + 8)
        for c in range(4):
            swap(QT, c, c)
        product(st, 10, 18, second_pair)
        pe.wait_ge(group_free, 2 + st.g + 16)
        for c in range(4):
            swap(KTL, c, 4 + c)
        product(st, 18, 24, second_pair)
        pe.wait_ge(group_free, 2 + st.g + 24)
        values((0, 1))

        def scores2(h):
            hh = DEPTH * HEADS + h
            part = slice(64 * (h % 2), 64 * (h % 2) + 64)
            for qb in range(TT):
                if h >= 2:
                    pe.wait_ge(exp_done, 2 * (hh - 2) + qb + 1)
                at = (h // 2) * T
                bank = banks[4 * (h % 2) + qb]
                q = arena[part, QT + at + qb * P:QT + at + (qb + 1) * P]
                pe.matmul(bank[:, 0:T], q, arena[part, KTL + at:KTL + at + T], start=True, stop=True)
                pe.matmul(bank[:, T:2 * T], q, arena[part, KTC + at:KTC + at + T], start=True,
                          stop=True).then_inc(scores_ready, 1)

        def turn_probs2(h):
            hh = DEPTH * HEADS + h
            pe.wait_ge(probs_ready, 2 * hh + 2)
            for half in range(2):
                if h:
                    pe.wait_ge(pt_copied, 2 * 8 + 2 * (h - 1) + half + 1)
                for kt in (2 * half, 2 * half + 1):
                    for qb in range(TT):
                        last = pe.transpose(banks[2 + half][:, (kt % 2) * T + qb * P:(kt % 2) * T + (qb + 1) * P],
                                            A(PR2 + (h % 2) * 1024 + qb * 512 + kt * P, P), ident[:, :])
                last.then_inc(transposed, 1)

        pe.wait_ge(roped, 5 * DEPTH + 8)
        scores2(0)
        scores2(1)
        turn_probs2(0)
        for h in range(HEADS2):
            if h + 2 < HEADS2:
                scores2(h + 2)
            part = slice(64 * (h % 2), 64 * (h % 2) + 64)
            if h % 2 == 0 and h >= 4:
                pe.wait_ge(xl_ready, made["na_o"] - KT + (h - 4) // 2 + 1)
            if h == 0:
                pe.wait_ge(v_ready, 2 + 8)
            for kt in range(4):
                if kt % 2 == 0:
                    pe.wait_ge(pt_copied, 2 * 8 + 2 * h + kt // 2 + 1)
                last = pe.matmul(banks[6 + (h // 2) % 2][part, 0:T], A(VNAT + kt * D + h * HEAD_DIM2, HEAD_DIM2),
                                 A(PT2 + (h % 2) * 1024 + kt * T, T), start=kt == 0, stop=kt == 3)
            last.then_inc(pv_done, 1)
            if h + 1 < HEADS2:
                turn_probs2(h + 1)
        product(stages["na_o"])

        def stream_norm(semaphore, name):
            column_mean(X_, banks[6], semaphore, name)
            mean_square(ZSQ, banks[7])

        seen.at["group_free"] = 2 + stages["na_o"].g
        stream_norm(group_free, "group_free")
        pairs(stages["ffn.0.1"], 2)
        finish_acc()
        stream_norm(evacuated, "evacuated")
        pairs(stages["ffn.1.0"], 2)
        finish_acc()
        stream_norm(evacuated, "evacuated")
        product(stages["conv_in"])
        product(stages["conv_o"])
        seen.at["group_free"] = 2 + stages["conv_o"].g
        stream_norm(group_free, "group_free")
        pairs(stages["ffn.1.1"], 2)
        finish_acc()
        stream_norm(evacuated, "evacuated")


def shape_tables():
    at, n = table_places()
    out = np.zeros((P, n), np.float32)

    def put(name, value):
        a, w = at[name]
        out[:, a:a + w] = value

    put("ident", np.eye(P, dtype=np.float32))
    put("iota", np.arange(P, dtype=np.float32)[None])
    t = np.arange(T)
    row, col = (t // GRID_W).astype(np.float32), (t % GRID_W).astype(np.float32)

    def rope(prefix, head, inv):
        quarter = head // 4
        d = np.arange(P) % head
        half = d // (2 * quarter)
        freq = inv[d % quarter]
        ang = np.where(half[:, None] == 0, row[None], col[None]).astype(freq.dtype) * freq[:, None]
        second = (d // quarter) % 2
        put(f"cos{prefix}", np.cos(ang))
        put(f"sin{prefix}", np.sin(ang) * np.where(second == 1, 1.0, -1.0)[:, None].astype(ang.dtype))
        partner = np.arange(P) + np.where(second == 1, -quarter, quarter)
        swap = np.zeros((P, P), np.float32)
        swap[partner, np.arange(P)] = 1.0
        put(f"swap{prefix}", swap)

    inv1 = (1.0 / (np.float32(10000.0) ** (np.arange(0, 64, 2, dtype=np.float32) / np.float32(64)))).astype(np.float32)
    rope("1", HEAD_DIM, inv1)
    rope("2", HEAD_DIM2, 10000.0 ** (-np.arange(16) / 16))
    for name in ("cos2", "sin2"):
        a, w = at[name]
        put(name + "_q", out[:, a:a + w] * HEAD_DIM2 ** -0.5)
    counts = [np.clip(t + w // 2, 0, T) - np.clip(t - w // 2, 0, T) for w in POOL_WINDOWS]
    put("inv_count", np.concatenate([1.0 / c for c in counts])[None])
    qc, kc = np.arange(GRID_W)[:, None], np.arange(GRID_W)[None]
    first = np.clip(qc - NA_KW // 2, 0, GRID_W - NA_KW)
    ok = (kc >= first) & (kc < first + NA_KW)
    put("mask", np.tile(np.where(ok, 0.0, MASKED), (2, 1)))
    return out


def tile_units(w):
    n = w.shape[1] // P
    return w.reshape(KT, P, n, P).transpose(2, 1, 0, 3).reshape(n, P, UNIT)


def row_units(w):
    return w.reshape(KT, P, -1, UNIT).transpose(2, 0, 1, 3).reshape(-1, P, UNIT)


def fill_stream(i):
    stages, placed = plan()
    stream = np.empty((placed, P, UNIT), np.float32)

    def put(name, units):
        at = stages[name].source
        stream[at:at + len(units)] = units

    for l in range(DEPTH):
        put(f"ada1.{l}", row_units(i["ada_w"][l]))
        put(f"w_in.{l}", tile_units(i["w_in"][l]))
        put(f"attn_o.{l}", tile_units(i["w_attn_o"][l]))
        mix = np.zeros((1, P, UNIT), np.float32)
        mix[0, :, :POOL_GROUPS * P] = i["pool_mix_w"][l].transpose(1, 0, 2).reshape(P, -1)
        put(f"pool_mix.{l}", mix)
        put(f"pool_o.{l}", i["w_pool_o"][l].reshape(POOL_GROUPS, P, UNIT))
        put(f"w_out.{l}", tile_units(i["w_out"][l]))
        put(f"query.{l}", tile_units(i["w_query"][l]))
        put(f"sub_keys.{l}", i["sub_keys"][l].reshape(4, 4, KEYS, 2, P).transpose(0, 4, 1, 3, 2).reshape(4, P, UNIT))
        at = stages[f"experts.{l}"].source
        u = i["expert_u"][l].reshape(KEYS, KEYS, KT, P).transpose(1, 3, 2, 0).reshape(KEYS, P, UNIT)
        v = i["expert_v"][l].reshape(KEYS, KEYS, UNIT).transpose(1, 0, 2)
        j = np.arange(KEYS)
        stream[at + np.where(j == 0, 0, 2 * j - 1)] = u
        stream[at + np.where(j == KEYS - 1, 2 * KEYS - 1, 2 * j + 2)] = v
        for k in range(2):
            at = stages[f"ffn.{l}.{k}"].source
            w = tile_units(i["ffn_w_in_2"][l, k])
            f = np.arange(FF_TILES)
            first = np.where(f == 0, 0, 3 * f - 1)
            stream[at + first] = w[:FF_TILES]
            stream[at + first + 1] = w[FF_TILES:]
            stream[at + np.where(f == FF_TILES - 1, 3 * FF_TILES - 1, 3 * f + 4)] = \
                i["ffn_w_out_2"][l, k].reshape(FF_TILES, P, UNIT)
    ada2 = np.concatenate([row_units(i["ada_w_2"][l]) for l in range(DEPTH)])
    for l in range(DEPTH):
        first = KT * ADA2_FIRST[l]
        middle, end = first + KT * ADA2_CHOICE[l], first + KT * (ADA2_CHOICE[l] + ADA2_GATES)
        if middle > first:
            put(f"ada2_choice.{l}", ada2[first:middle])
        put(f"ada2_gates.{l}", ada2[middle:end])
    put("qkv", tile_units(i["na_w_qkv_2"][0]))
    put("na_o", tile_units(i["na_w_out_2"][0]))
    put("conv_in", tile_units(i["sc_w_in_2"][0]))
    put("conv_o", tile_units(i["sc_w_out_2"][0]))
    return stream


def fill_columns(i):
    at, n = column_places()
    out = np.empty((P, n), np.float32)

    def put(name, v):
        a, w = at[name]
        out[:, a:a + w] = np.asarray(v).reshape(w, P).T

    put("c", i["c"])
    put("c_2", i["c_2"])
    put("c_ctx", i["c_ctx_2"])
    put("final_norm", i["final_norm_w"])
    for l in range(DEPTH):
        put(f"ada_b.{l}", i["ada_b"][l])
        put(f"norm_mix.{l}", i["norm_mix_w"][l])
        put(f"norm_ffn.{l}", i["norm_ffn_w"][l])
        put(f"q_norm.{l}", i["q_norm_w"][l])
        put(f"k_norm.{l}", i["k_norm_w"][l])
        put(f"pool_scale.{l}", i["pool_scale"][l])
        put(f"ada_b_2.{l}", i["ada_b_2"][l])
        for k in range(3):
            put(f"ln_g.{l}.{k}", i["ln_g_2"][l, k])
            put(f"ln_b.{l}.{k}", i["ln_b_2"][l, k])
    for k in range(3):
        put(f"conv.{k}", i["sc_conv_2"][0, k])
    return out


def transposed_tokens(x):
    return np.ascontiguousarray(x[0].T.reshape(KT, P, T).transpose(1, 0, 2))


def skewed_bias(rpb):
    pad = GRID_W - NA_KW
    padded = np.zeros((HEADS2, RPB_H, RPB_W + 2 * pad), np.float32)
    padded[:, :, pad:pad + RPB_W] = rpb
    rows = [padded[:, :, GRID_W - 1 - qc:2 * GRID_W - 1 - qc] for qc in range(GRID_W)]
    return np.stack(rows).reshape(GRID_W, HEADS2, RPB_H * GRID_W)


def kernel(**inputs):
    from contextlib import ExitStack

    import concourse.bacc as bacc
    from concourse.bass_utils import run_bass_kernel_spmd

    i = {k: np.asarray(v) for k, v in inputs.items()}
    arrays = {
        "stream": fill_stream(i), "columns": fill_columns(i), "tables": shape_tables(),
        "x_t": transposed_tokens(i["x"]), "ctx_t": transposed_tokens(i["ctx_2"]), "rpb": skewed_bias(i["na_rpb_2"][0]),
    }
    nc = bacc.Bacc("TRN2", target_bir_lowering=False, num_devices=1)
    args = [nc.dram_tensor(name, a.shape, F32, kind="ExternalInput").ap() for name, a in arrays.items()]
    out = nc.dram_tensor("out_t", (P, KT, T), F32, kind="ExternalOutput").ap()
    with ExitStack() as ctx:
        build(nc, ctx, *args, out)
    r = run_bass_kernel_spmd(nc, [arrays], core_ids=[0])
    y = r.results[0]["out_t"]
    return np.ascontiguousarray(y.transpose(1, 0, 2).reshape(D, T).T)[None]
```
